# Optimizing a Trainium2 kernel written in Bass

```python
import math
import jax
import jax.numpy as jnp
from jax import lax
import numpy as np

D_MODEL = 1024
BATCH = 1
SEQ = 512
DEPTH = 2

GRID_W = 64
CTX_LEN = 256
EPS = 1e-6
N_MOD = 6

POOL_GROUPS = 4
POOL_GDIM = D_MODEL // 16
POOL_DIM = POOL_GROUPS * POOL_GDIM
POOL_WINDOWS = (2, 4, 8, 16)

SSD_HEADS = 4
SSD_HEAD_DIM = 64
SSD_INNER = SSD_HEADS * SSD_HEAD_DIM
SSD_GROUPS = 2
SSD_STATE = 64
SSD_CONV = 5
SSD_CHUNK = 128
SSD_DIRS = 2
SSD_XBC = SSD_INNER + 2 * SSD_GROUPS * SSD_STATE
SSD_PROJ = SSD_INNER + SSD_XBC + SSD_DIRS * SSD_HEADS

ATTN_HEADS = 4
ATTN_KV_HEADS = 2
HEAD_DIM = 128
ATTN_REP = ATTN_HEADS // ATTN_KV_HEADS
ATTN_DIM = ATTN_HEADS * HEAD_DIM
KV_DIM = ATTN_KV_HEADS * HEAD_DIM
ATTN_PROJ = ATTN_DIM + 2 * KV_DIM
Q_BLOCK = 128
ROPE_THETA = 10000.0

D_MIX = POOL_DIM + SSD_INNER + ATTN_DIM
D_IN = POOL_DIM + SSD_PROJ + ATTN_PROJ
D_FF = -(-(8 * D_MODEL) // (3 * 256)) * 256

kernel_name = 'hybrid_pool_ssd_gqa_dit_block'

def rmsnorm(x, w):
    xf = x.astype(jnp.float32)
    xf = xf * lax.rsqrt(jnp.mean(xf * xf, axis=-1, keepdims=True) + EPS)
    return xf.astype(x.dtype) * w

def modulation(cond, w_mod, b_mod):
    m = jax.nn.silu(cond) @ w_mod + b_mod
    return [t[:, None, :] for t in jnp.split(m, N_MOD, axis=-1)]

def adaln(h, w, shift, scale):
    return rmsnorm(h, w) * (1 + scale) + shift

def centred_mean_minus_self(u, w):
    L = u.shape[1]
    cs = jnp.cumsum(u.astype(jnp.float32), axis=1)
    cs = jnp.concatenate([jnp.zeros_like(cs[:, :1]), cs], axis=1)
    t = jnp.arange(L)
    lo = jnp.clip(t - w // 2, 0, L)
    hi = jnp.clip(t - w // 2 + w, 0, L)
    cnt = (hi - lo).astype(jnp.float32)[None, :, None]
    mean = (jnp.take(cs, hi, axis=1) - jnp.take(cs, lo, axis=1)) / cnt
    return mean.astype(u.dtype) - u

def pool_mixer(u, pool_w, pool_scale):
    Bsz, L, _ = u.shape
    ug = u.reshape(Bsz, L, POOL_GROUPS, POOL_GDIM)
    pooled = jnp.stack([centred_mean_minus_self(ug[:, :, g], w) for g, w in enumerate(POOL_WINDOWS)], axis=2)
    out = jnp.einsum('blgc,gcd->blgd', pooled, pool_w).reshape(Bsz, L, POOL_DIM)
    return out * pool_scale

def dwconv_centred(u, w, b):
    pad = w.shape[0] // 2
    out = lax.conv_general_dilated(u, w[:, None, :].astype(u.dtype), window_strides=(1,),
                                   padding=[(pad, pad)], dimension_numbers=('NWC', 'WIO', 'NWC'),
                                   feature_group_count=u.shape[-1])
    return out + b

def ssd_prep(u, conv_w, conv_b):
    Bsz, L, _ = u.shape
    z = u[..., :SSD_INNER]
    xbc = jax.nn.silu(dwconv_centred(u[..., SSD_INNER:SSD_INNER + SSD_XBC], conv_w, conv_b))
    xh = xbc[..., :SSD_INNER].reshape(Bsz, L, SSD_HEADS, SSD_HEAD_DIM)
    bc = xbc[..., SSD_INNER:].reshape(Bsz, L, 2, SSD_GROUPS, SSD_STATE)
    rep = SSD_HEADS // SSD_GROUPS
    Bm = jnp.repeat(bc[:, :, 0], rep, axis=2)
    Cm = jnp.repeat(bc[:, :, 1], rep, axis=2)
    dt_raw = u[..., SSD_INNER + SSD_XBC:].reshape(Bsz, L, SSD_DIRS, SSD_HEADS)
    return z, xh, Bm, Cm, dt_raw

def segsum(a):
    T = a.shape[-1]
    cs = jnp.cumsum(a, axis=-1)
    diff = cs[..., :, None] - cs[..., None, :]
    mask = jnp.tril(jnp.ones((T, T), dtype=bool))
    return jnp.where(mask, diff, -jnp.inf)

def ssd_scan(xh, dt, A, Bm, Cm, h0, with_output):
    Bsz, L, H, P = xh.shape
    N = Bm.shape[-1]
    nc = L // SSD_CHUNK
    x = (xh * dt[..., None]).reshape(Bsz, nc, SSD_CHUNK, H, P)
    a = (dt * A).reshape(Bsz, nc, SSD_CHUNK, H).transpose(0, 3, 1, 2)
    Bc = Bm.reshape(Bsz, nc, SSD_CHUNK, H, N)
    Cc = Cm.reshape(Bsz, nc, SSD_CHUNK, H, N)
    a_cs = jnp.cumsum(a, axis=-1)
    decay_states = jnp.exp(a_cs[..., -1:] - a_cs)
    states = jnp.einsum('bclhn,bhcl,bclhp->bchpn', Bc, decay_states, x)
    states = jnp.concatenate([h0[:, None].astype(states.dtype), states], axis=1)
    chunk_decay = jnp.exp(segsum(jnp.pad(a_cs[..., -1], ((0, 0), (0, 0), (1, 0)))))
    new_states = jnp.einsum('bhzc,bchpn->bzhpn', chunk_decay, states)
    prev_states, final = new_states[:, :-1], new_states[:, -1]
    if not with_output:
        return None, final
    Lmat = jnp.exp(segsum(a))
    scores = jnp.einsum('bclhn,bcshn->bhcls', Cc, Bc) * Lmat
    y_diag = jnp.einsum('bhcls,bcshp->bclhp', scores, x)
    y_off = jnp.einsum('bclhn,bchpn,bhcl->bclhp', Cc, prev_states, jnp.exp(a_cs))
    return (y_diag + y_off).reshape(Bsz, L, H, P), final

def gated_rmsnorm(y, z, w):
    Bsz, L = y.shape[:2]
    g = (y.reshape(Bsz, L, SSD_INNER) * jax.nn.silu(z.astype(jnp.float32))).reshape(Bsz, L, SSD_GROUPS, -1)
    g = g * lax.rsqrt(jnp.mean(g * g, axis=-1, keepdims=True) + EPS)
    return g.reshape(Bsz, L, SSD_INNER).astype(z.dtype) * w

def ssd_bidirectional(pc, px, dt_bias, a_log, d_skip, ssd_norm_w, need_ctx):
    zc, xc, Bc, Cc, dtc = pc
    zx, xx, Bx, Cx, dtx = px
    Bsz = xx.shape[0]
    y_x = jnp.zeros(xx.shape, jnp.float32)
    y_c = jnp.zeros(xc.shape, jnp.float32)
    for d in range(SSD_DIRS):
        flip = (lambda t: jnp.flip(t, axis=1)) if d == 1 else (lambda t: t)
        A = -jnp.exp(a_log[d].astype(jnp.float32))
        dt_c = jax.nn.softplus(dtc[:, :, d].astype(jnp.float32) + dt_bias[d])
        dt_x = jax.nn.softplus(dtx[:, :, d].astype(jnp.float32) + dt_bias[d])
        h0 = jnp.zeros((Bsz, SSD_HEADS, SSD_HEAD_DIM, SSD_STATE), jnp.float32)
        yc_d, hc = ssd_scan(flip(xc), flip(dt_c), A, flip(Bc), flip(Cc), h0, need_ctx)
        yx_d, _ = ssd_scan(flip(xx), flip(dt_x), A, flip(Bx), flip(Cx), hc, True)
        y_x = y_x + flip(yx_d) + d_skip[d][:, None] * xx
        if need_ctx:
            y_c = y_c + flip(yc_d) + d_skip[d][:, None] * xc
    out_x = gated_rmsnorm(y_x, zx, ssd_norm_w)
    out_c = gated_rmsnorm(y_c, zc, ssd_norm_w) if need_ctx else None
    return out_c, out_x

def axial_rope_tables(L):
    rows = L // GRID_W
    row_ids = jnp.repeat(jnp.arange(rows, dtype=jnp.float32), GRID_W)
    col_ids = jnp.tile(jnp.arange(GRID_W, dtype=jnp.float32), rows)
    axis_dim = HEAD_DIM // 2
    inv_freq = ROPE_THETA ** (-jnp.arange(0, axis_dim, 2, dtype=jnp.float32) / axis_dim)
    ang_r = row_ids[:, None] * inv_freq[None, :]
    ang_c = col_ids[:, None] * inv_freq[None, :]
    return jnp.cos(ang_r), jnp.sin(ang_r), jnp.cos(ang_c), jnp.sin(ang_c)

def rope_half(x, cos, sin):
    m = x.shape[-1] // 2
    x1, x2 = x[..., :m], x[..., m:]
    cos = cos[:, None, :].astype(x.dtype)
    sin = sin[:, None, :].astype(x.dtype)
    return jnp.concatenate([x1 * cos - x2 * sin, x1 * sin + x2 * cos], axis=-1)

def apply_axial_rope(x, tables):
    cr, sr, cc, sc = tables
    h = HEAD_DIM // 2
    return jnp.concatenate([rope_half(x[..., :h], cr, sr), rope_half(x[..., h:], cc, sc)], axis=-1)

def attn_split(u, q_norm_w, k_norm_w):
    Bsz, L, _ = u.shape
    q = rmsnorm(u[..., :ATTN_DIM].reshape(Bsz, L, ATTN_HEADS, HEAD_DIM), q_norm_w)
    k = rmsnorm(u[..., ATTN_DIM:ATTN_DIM + KV_DIM].reshape(Bsz, L, ATTN_KV_HEADS, HEAD_DIM), k_norm_w)
    v = u[..., ATTN_DIM + KV_DIM:].reshape(Bsz, L, ATTN_KV_HEADS, HEAD_DIM)
    return q, k, v

def gqa_attend(qblk, k, v):
    s = jnp.einsum('bqgrd,bkgd->bgrqk', qblk, k).astype(jnp.float32) * (HEAD_DIM ** -0.5)
    p = jax.nn.softmax(s, axis=-1).astype(v.dtype)
    return jnp.einsum('bgrqk,bkgd->bqgrd', p, v)

def latent_attention(q, k_all, v_all):
    Bsz, L = q.shape[:2]
    nb = L // Q_BLOCK
    qb = q.reshape(Bsz, nb, Q_BLOCK, ATTN_KV_HEADS, ATTN_REP, HEAD_DIM).transpose(1, 0, 2, 3, 4, 5)
    out = lax.map(lambda qblk: gqa_attend(qblk, k_all, v_all), qb)
    return out.transpose(1, 0, 2, 3, 4, 5).reshape(Bsz, L, ATTN_DIM)

def context_attention(q, k, v):
    Bsz, L = q.shape[:2]
    qg = q.reshape(Bsz, L, ATTN_KV_HEADS, ATTN_REP, HEAD_DIM)
    return gqa_attend(qg, k, v).reshape(Bsz, L, ATTN_DIM)

def swiglu(h, w1, w3, w2):
    return (jax.nn.silu(h @ w1) * (h @ w3)) @ w2

def hybrid_layer(xs, cs, c, c_ctx, norm1_w, norm2_w, w_mod, b_mod, w_in, pool_w, pool_scale,
                 conv_w, conv_b, dt_bias, a_log, d_skip, ssd_norm_w, q_norm_w, k_norm_w,
                 w_out, w1, w3, w2, rope, need_ctx):
    sh1x, sc1x, g1x, sh2x, sc2x, g2x = modulation(c, w_mod, b_mod)
    sh1c, sc1c, g1c, sh2c, sc2c, g2c = modulation(c_ctx[None, :], w_mod, b_mod)
    ux = adaln(xs, norm1_w, sh1x, sc1x) @ w_in
    uc = adaln(cs, norm1_w, sh1c, sc1c) @ w_in
    o_ssd, o_att = POOL_DIM, POOL_DIM + SSD_PROJ

    pool_x = pool_mixer(ux[..., :o_ssd], pool_w, pool_scale)
    ssd_c, ssd_x = ssd_bidirectional(ssd_prep(uc[..., o_ssd:o_att], conv_w, conv_b),
                                     ssd_prep(ux[..., o_ssd:o_att], conv_w, conv_b),
                                     dt_bias, a_log, d_skip, ssd_norm_w, need_ctx)
    qx, kx, vx = attn_split(ux[..., o_att:], q_norm_w, k_norm_w)
    qc, kc, vc = attn_split(uc[..., o_att:], q_norm_w, k_norm_w)
    qx = apply_axial_rope(qx, rope)
    kx = apply_axial_rope(kx, rope)
    attn_x = latent_attention(qx, jnp.concatenate([kc, kx], axis=1), jnp.concatenate([vc, vx], axis=1))

    mix_x = jnp.concatenate([pool_x, ssd_x.astype(xs.dtype), attn_x], axis=-1) @ w_out
    xs = xs + g1x * mix_x
    xs = xs + g2x * swiglu(adaln(xs, norm2_w, sh2x, sc2x), w1, w3, w2)

    if need_ctx:
        pool_c = pool_mixer(uc[..., :o_ssd], pool_w, pool_scale)
        attn_c = context_attention(qc, kc, vc)
        mix_c = jnp.concatenate([pool_c, ssd_c.astype(cs.dtype), attn_c], axis=-1) @ w_out
        cs = cs + g1c * mix_c
        cs = cs + g2c * swiglu(adaln(cs, norm2_w, sh2c, sc2c), w1, w3, w2)
    return xs, cs

def setup_inputs(seed: int = 0) -> dict:
    key = jax.random.key(seed)
    ks = jax.random.split(key, 24)
    f32 = jnp.float32

    def nrm(k, shape, scale):
        return jax.random.normal(k, shape, f32) * scale

    dt0 = jnp.exp(jax.random.uniform(ks[13], (DEPTH, SSD_DIRS, SSD_HEADS), f32, math.log(1e-3), math.log(1e-1)))
    return {
        'x': nrm(ks[0], (BATCH, SEQ, D_MODEL), 1.0),
        'c': nrm(ks[1], (BATCH, D_MODEL), 1.0),
        'ctx': nrm(ks[2], (BATCH, CTX_LEN, D_MODEL), 1.0),
        'c_ctx': nrm(ks[3], (D_MODEL,), 1.0),
        'norm1_w': 1.0 + nrm(ks[4], (DEPTH, D_MODEL), 0.05),
        'norm2_w': 1.0 + nrm(ks[5], (DEPTH, D_MODEL), 0.05),
        'w_mod': nrm(ks[6], (DEPTH, D_MODEL, N_MOD * D_MODEL), 0.5 * D_MODEL ** -0.5),
        'b_mod': nrm(ks[7], (DEPTH, N_MOD * D_MODEL), 0.02),
        'w_in': nrm(ks[8], (DEPTH, D_MODEL, D_IN), D_MODEL ** -0.5),
        'pool_w': nrm(ks[9], (DEPTH, POOL_GROUPS, POOL_GDIM, POOL_GDIM), POOL_GDIM ** -0.5),
        'pool_scale': 1.0 + nrm(ks[10], (DEPTH, POOL_DIM), 0.1),
        'conv_w': nrm(ks[11], (DEPTH, SSD_CONV, SSD_XBC), SSD_CONV ** -0.5),
        'conv_b': nrm(ks[12], (DEPTH, SSD_XBC), 0.02),
        'dt_bias': dt0 + jnp.log(-jnp.expm1(-dt0)),
        'a_log': jnp.log(jax.random.uniform(ks[14], (DEPTH, SSD_DIRS, SSD_HEADS), f32, 1.0, 16.0)),
        'd_skip': 1.0 + nrm(ks[15], (DEPTH, SSD_DIRS, SSD_HEADS), 0.1),
        'ssd_norm_w': 1.0 + nrm(ks[16], (DEPTH, SSD_INNER), 0.05),
        'q_norm_w': 1.0 + nrm(ks[17], (DEPTH, HEAD_DIM), 0.05),
        'k_norm_w': 1.0 + nrm(ks[18], (DEPTH, HEAD_DIM), 0.05),
        'w_out': nrm(ks[19], (DEPTH, D_MIX, D_MODEL), D_MIX ** -0.5),
        'w1': nrm(ks[20], (DEPTH, D_MODEL, D_FF), D_MODEL ** -0.5),
        'w3': nrm(ks[21], (DEPTH, D_MODEL, D_FF), D_MODEL ** -0.5),
        'w2': nrm(ks[22], (DEPTH, D_FF, D_MODEL), D_FF ** -0.5),
    }

def reference(x, c, ctx, c_ctx, norm1_w, norm2_w, w_mod, b_mod, w_in, pool_w, pool_scale,
              conv_w, conv_b, dt_bias, a_log, d_skip, ssd_norm_w, q_norm_w, k_norm_w,
              w_out, w1, w3, w2):
    rope = axial_rope_tables(x.shape[1])
    xs, cs = x, ctx
    for layer in range(DEPTH):
        xs, cs = hybrid_layer(xs, cs, c, c_ctx, norm1_w[layer], norm2_w[layer], w_mod[layer], b_mod[layer],
                              w_in[layer], pool_w[layer], pool_scale[layer], conv_w[layer], conv_b[layer],
                              dt_bias[layer], a_log[layer], d_skip[layer], ssd_norm_w[layer],
                              q_norm_w[layer], k_norm_w[layer], w_out[layer], w1[layer], w3[layer], w2[layer],
                              rope, need_ctx=(layer < DEPTH - 1))
    return xs


_drawn_inputs = setup_inputs


def setup_inputs(seed=0):
    import zlib

    import numpy as np

    out = dict(_drawn_inputs(seed))
    spreads = {}
    factors = {'ctx': 4.852,
     'norm1_w': 3.055,
     'pool_scale': 2.761,
     'conv_b': 8.0,
     'd_skip': 8.0,
     'ssd_norm_w': 5.096,
     'q_norm_w': 8.0,
     'k_norm_w': 8.0}
    for name, (base, spread) in spreads.items():
        noise = np.random.default_rng([zlib.crc32(name.encode()), seed]).standard_normal(out[name].shape)
        drawn = base * np.exp(spread * noise) if base else spread * noise
        out[name] = jnp.asarray(drawn.astype(out[name].dtype))
    for name, factor in factors.items():
        out[name] = (out[name] * factor).astype(out[name].dtype)
    return out
```

```python
from contextlib import ExitStack

import numpy as np

import concourse.bass as bass
from concourse import mybir

ALU = mybir.AluOpType
ACT = mybir.ActivationFunctionType
F32 = mybir.dt.float32
F32R = mybir.dt.float32r
AX_X = mybir.AxisListType.X

P = 128
D = 1024
KC = D // P
CTX, SEQ = 256, 512
T = CTX + SEQ
TT = T // P
DEPTH = 2
EPS = 1e-6
GRID_W = 64
N_MOD = 6
POOL_DIM = 256
SSD_INNER = 256
HEADS = 4
HD_SSD = 64
DIRS = 2
ATT_HEADS, KV_HEADS, HEAD_DIM = 4, 2, 128
D_FF = 2816
OFF_POOL, OFF_Z, OFF_XBC, OFF_TOK = 0, 256, 512, 1024
N_DT = DIRS * HEADS
D_IN = OFF_TOK + N_DT + ATT_HEADS * HEAD_DIM + 2 * KV_HEADS * HEAD_DIM
PAD = 8
PW = PAD + CTX + 2 * PAD + SEQ + PAD
PC0, PL0 = PAD, PAD + CTX + 2 * PAD
POOL_WINDOWS = (2, 4, 8, 16)

N_FEAT = 8
N_TOK = 8
N_OUT = 8
FF_BLOCKS = (8, 8, 6)
N_TILES = N_FEAT + N_TOK + N_OUT + sum(2 * f + KC for f in FF_BLOCKS)
WT = 4 * 264
FEAT_COLS = (0, 128, 512, 640, 768, 896, 256, 384)
V_BMOD, V_N1, V_N2, V_PS, V_CB, V_CW, V_SN, V_C = 0, 48, 56, 64, 66, 70, 90, 92
N_VEC = (V_C + 2 * KC, V_C)

UNITS = ATT_HEADS * (SEQ // P + 1)
TR_A = 2 + 1 + KV_HEADS + ATT_HEADS + UNITS
TR_B = TR_A - ATT_HEADS
STATES = DIRS * (TT - 1)
INCS = dict(
    sq_ready=KC, acc_ready=KC - 2, ss_ready=1, root_ready=1, rstd_ready=1, t_ready=KC, h_hi_ready=KC,
    h_lo_ready=KC, xbc_ready=5, pads_zero=8, count_used=2, pooled_ready=2, qksq_ready=3, qkss_ready=3,
    qkrt_ready=3, qkn_ready=3, rope_s_ready=6, qk_ready=3, dt_in=1, dt_exp=2, a_ready=1, cs_pe=1, cs_ready=3,
    ws_ready=1, trA=TR_A, trA_out=TR_A, trB=TR_B, trB_out=TR_B, xw_ready=STATES, st_pe=STATES, st_ready=STATES,
    pm_pe=2, pm_out=2, s_ready=UNITS, max_ready=UNITS, exp_ready=UNITS, p_ready=UNITS, pv_pe=UNITS,
    pv_out=2 * ATT_HEADS, g_pe=TT, cb_pe=2 * TT, gm_ready=2 * TT, d_ready=TT, d_back_ready=TT, ecum_ready=2 * TT,
    e_ready=2 * TT, w_ready=TT, w_back_ready=TT, cdec_ready=2 * TT, xdt_ready=2 * TT, y_pe=TT, y_out=2 * TT, gz_ready=2,
    gsq_ready=2, gss_pe=4, gss_out=4, groot_ready=1, gn_done=6, m_hi_ready=KC, m_lo_ready=KC,
)


def shape_constants():
    j = np.arange(P)
    ident = np.eye(P)
    le = (j[:, None] <= j[None, :]).astype(np.float64)
    ge = (j[:, None] >= j[None, :]).astype(np.float64)
    gt = (j[:, None] > j[None, :]).astype(np.float64)
    lt = (j[:, None] < j[None, :]).astype(np.float64)
    ones = np.ones((P, P))
    axis_dim = HEAD_DIM // 2
    inv = 10000.0 ** (-np.arange(0, axis_dim, 2) / axis_dim)
    t = np.arange(SEQ)
    ang = np.stack([(t // GRID_W)[:, None] * inv, (t % GRID_W)[:, None] * inv], 1)
    cos, sin = np.cos(ang), np.sin(ang)
    rc = np.concatenate([cos, cos], 2).reshape(SEQ, HEAD_DIM)
    rs = np.concatenate([-sin, sin], 2).reshape(SEQ, HEAD_DIM)
    rc = np.tile(rc.reshape(SEQ // P, P, 1, HEAD_DIM).transpose(1, 0, 2, 3), (1, 1, 2, 1)).reshape(P, -1)
    rs = np.tile(rs.reshape(SEQ // P, P, 1, HEAD_DIM).transpose(1, 0, 2, 3), (1, 1, 2, 1)).reshape(P, -1)
    table = np.concatenate([ident, le, ge, gt, lt, ones, rc, rs], 1).astype(np.float32)
    count = np.zeros((2, P, PW), np.float32)
    for f in range(2):
        for half in range(2):
            w = POOL_WINDOWS[2 * f + half]
            for start, n in ((PC0, CTX), (PL0, SEQ)):
                t = np.arange(n)
                lo, hi = np.clip(t - w // 2, 0, n), np.clip(t - w // 2 + w, 0, n)
                count[f, 64 * half:64 * half + 64, start:start + n] = 1.0 / (hi - lo)
    return table, count


class OwnOrder:

    def __init__(self, sem):
        self.sem, self.n, self.i, self.per, self.base = sem, 0, None, 0, 0

    def loop(self, i, per):
        self.i, self.per, self.base = i, per, self.n

    def end(self, count):
        assert self.n - self.base == self.per, (self.n - self.base, self.per)
        self.n, self.i = self.base + self.per * count, None

    def mark(self, ins):
        ins.then_inc(self.sem, 1)
        self.n += 1
        return self.n if self.i is None else self.i * self.per + self.n


def hybrid_kernel(nc, x, c, ctx, c_ctx, norm1_w, norm2_w, w_mod, b_mod, w_in, pool_w, pool_scale, conv_w,
                  conv_b, dt_bias, a_log, d_skip, ssd_norm_w, q_norm_w, k_norm_w, w_out, w1, w3, w2,
                  table, count, out):
    with ExitStack() as stack:
        usable = nc.sbuf_usable_end - nc.sbuf_base - 64
        stack.enter_context(nc.sbuf_tensor("arena", [P, usable // 4], F32))
        start = -(-(nc.sbuf_usable_end - usable) // 64) * 64
        start = (nc.sbuf_base - (usable // 4) * 4) // 64 * 64 + 64
        place = [start]

        def put(name, shape, dt=F32, at=None):
            size = 4 * int(np.prod(shape[1:]))
            if at is None:
                at, place[0] = place[0], place[0] + (size + 31) // 32 * 32
            assert at + size <= nc.sbuf_usable_end, (name, at, size)
            return nc.alloc_sbuf_tensor_at(name, shape, dt, offset=at)

        x_res = put("x_res", [P, KC, T])
        H0 = place[0]
        h_hi = put("h_hi", [P, KC, T], F32R)
        h_lo = put("h_lo", [P, KC, T], F32R)
        raw = [put(f"raw{s}", [P, WT]) for s in range(4)]
        w_hi = [put(f"w_hi{s}", [P, WT], F32R) for s in range(2)]
        w_lo = [put(f"w_lo{s}", [P, WT], F32R) for s in range(2)]
        M0 = place[0]
        mod_ring = [put(f"mod_ring{s}", [P, D]) for s in range(4)]
        tab = put("tab", [P, 6 * P + 2048])
        ident, tri_le, tri_ge, tri_gt, tri_lt, ones = (tab[:, i * P:(i + 1) * P] for i in range(6))
        rope_c, rope_s = tab[:, 768:1792], tab[:, 1792:2816]
        vecs = [put(f"vecs{l}", [P, 112]) for l in range(DEPTH)]
        cond = put("cond", [P, 2, KC])
        mod_rows = put("mod_rows", [P, 256])
        mods = [put(f"mods{l}", [P, N_MOD, 2, KC]) for l in range(DEPTH)]
        gain = [put(f"gain{l}", [P, 2, 2, KC]) for l in range(DEPTH)]
        dt_b = [put(f"dt_b{l}", [P, N_DT]) for l in range(DEPTH)]
        neg_a = [put(f"neg_a{l}", [P, N_DT]) for l in range(DEPTH)]
        qk_w = [put(f"qk_w{l}", [P, 2, HEAD_DIM]) for l in range(DEPTH)]
        skip2 = [put(f"skip2{l}", [P, 2 * HEADS]) for l in range(DEPTH)]
        skip = [put(f"skip{l}", [P, 2]) for l in range(DEPTH)]
        pool_bd = [put(f"pool_bd{l}", [P, 2, P]) for l in range(DEPTH)]
        eps = put("eps", [P, 1])
        dt_raw = put("dt_raw", [P, TT, N_DT])
        dt_m = put("dt_m", [P, TT, N_DT])
        dt_n = put("dt_n", [P, TT, N_DT])
        dts = put("dts", [P, TT, N_DT])
        a_tok = put("a_tok", [P, TT, N_DT])
        cs_tok = put("cs_tok", [P, DIRS, TT, HEADS])
        decay = put("decay", [P, DIRS, TT, HEADS])
        decay_all = put("decay_all", [P, TT, N_DT])
        w_state = put("w_state", [P, DIRS, TT, HEADS])
        qk_ss = put("qk_ss", [P, 3, 12])
        qk_rt = put("qk_rt", [P, 3, 12])
        neg_max = put("neg_max", [P, 2, 2])
        p_sum = put("p_sum", [P, 2, 2])
        p_inv = put("p_inv", [P, 2, 2])
        G0 = place[0]
        qk = put("qk", [P, 3, TT, 256])
        v_tok = put("v_tok", [P, TT, 256])
        silu_z = put("silu_z", [P, 2, T])
        b_T = put("b_T", [P, T])
        c_T = put("c_T", [P, 2, T])
        X0 = place[0]
        x_tok = put("x_tok", [P, TT, 256])
        b_tok = put("b_tok", [P, TT, P])
        MX0 = place[0]
        mix = put("mix", [P, 8, T])
        END = place[0]
        conv_acc = put("conv_acc", [P, 2, T], at=X0)
        qk_sq = put("qk_sq", [P, 12, P], at=X0)
        pool_u = put("pool_u", [P, 2, PW], at=MX0)
        win_a = put("win_a", [P, PW], at=MX0 + 8 * PW)
        win_b = put("win_b", [P, PW], at=MX0 + 12 * PW)
        inv_n = put("inv_n", [P, PW], at=MX0 + 16 * PW)
        rope_t = put("rope_t", [P, 1024], at=MX0 + 8 * PW)
        x_T = put("x_T", [P, 2, T], at=MX0 + 6 * 4 * T)
        assert 20 * PW <= 6 * 4 * T
        g_hi = put("g_hi", [P, 8 * T], F32R, at=G0)
        g_lo = put("g_lo", [P, 8 * T], F32R, at=G0 + 32 * T)
        silu_a = put("silu_a", [P, T], at=G0 + 64 * T)
        g_f = put("g_f", [P, 2, T], at=G0 + 68 * T)
        N0 = END - 24 * T
        assert N0 >= G0 + 48 * T and N0 >= X0
        sq = put("sq", [P, 2, T], at=N0)
        sq_acc = put("sq_acc", [P, T], at=N0 + 8 * T)
        rstd = put("rstd", [P, T], at=N0 + 12 * T)
        nrm = put("nrm", [P, 2, T], at=N0 + 16 * T)
        assert G0 + 76 * T <= END
        x_in = put("x_in", [P, TT, D], at=G0)
        vrows = [put(f"vrows{l}", [P, P], at=G0 + 4 * TT * D + 512 * l) for l in range(DEPTH)]
        x_out = put("x_out", [P, SEQ // P, D], at=G0)
        p_T = put("p_T", [P, 2, TT, P], at=H0)
        k_T = put("k_T", [P, KV_HEADS, T], at=H0 + 12288)
        q_T = put("q_T", [P, 2, T], at=H0 + 18432)
        S0 = H0 + 24576
        probs = put("probs", [P, 3, T], at=S0)
        e_in = put("e_in", [P, DIRS, HEADS, P], at=S0 + 9216)
        e_cum = put("e_cum", [P, DIRS, HEADS, P], at=S0 + 13312)
        g_mask = put("g_mask", [P, DIRS, 2, P], at=S0 + 17408)
        x_dt = put("x_dt", [P, DIRS, 256], at=S0 + 19456)
        x_w = put("x_w", [P, 2, 256], at=S0 + 21504)
        gn_sq = put("gn_sq", [P, T], at=S0 + 9216)
        gn_r = put("gn_r", [P, 2, T], at=S0 + 12288)
        h_prev = put("h_prev", [P, DIRS, TT, 256], at=M0)

        banks = stack.enter_context(nc.psum_tensor("banks", [P, 8, 512], F32))
        flat = banks[:, :, :].rearrange("p b n -> p (b n)")

        def sem(name):
            return stack.enter_context(nc.semaphore(name))

        raw_landed = [sem(f"raw_landed{s}") for s in range(4)]
        mod_landed = [sem(f"mod_landed{s}") for s in range(4)]
        vrows_landed = [sem(f"vrows_landed{l}") for l in range(DEPTH)]
        ident_landed, table_landed = sem("ident_landed"), sem("table_landed")
        x_landed = [sem(f"x_landed{t}") for t in range(TT)]
        small_landed = sem("small_landed")
        count_landed = sem("count_landed")
        out_stored = sem("out_stored")
        hi_ready, lo_ready, tile_done = sem("hi_ready"), sem("lo_ready"), sem("tile_done")
        pair_free = [sem("pair_free0"), sem("pair_free1")]
        tok_ready, tok_free = sem("tok_ready"), sem("tok_free")
        g_hi_ready, g_lo_ready = sem("g_hi_ready"), sem("g_lo_ready")
        mod_used, rows_ready, rows_T, mods_ready, gain_ready = (
            sem(n) for n in ("mod_used", "rows_ready", "rows_T", "mods_ready", "gain_ready"))
        zeroed, vec_T, vec_ready, cond_ready = (sem(n) for n in ("zeroed", "vec_T", "vec_ready", "cond_ready"))
        xT_pe, xT_a, xT_b, small_act, small_ready = (
            sem(n) for n in ("xT_pe", "xT_a", "xT_b", "small_act", "small_ready"))
        s_dve, s_act, s_pool = sem("dve_order"), sem("act_order"), sem("pool_order")
        sq_ready = sem("sq_ready")
        acc_ready = sem("acc_ready")
        ss_ready = sem("ss_ready")
        root_ready = sem("root_ready")
        rstd_ready = sem("rstd_ready")
        t_ready = sem("t_ready")
        h_hi_ready = sem("h_hi_ready")
        h_lo_ready = sem("h_lo_ready")
        xbc_ready = sem("xbc_ready")
        pads_zero = sem("pads_zero")
        count_used = sem("count_used")
        pooled_ready = sem("pooled_ready")
        qksq_ready = sem("qksq_ready")
        qkss_ready = sem("qkss_ready")
        qkrt_ready = sem("qkrt_ready")
        qkn_ready = sem("qkn_ready")
        rope_s_ready = sem("rope_s_ready")
        qk_ready = sem("qk_ready")
        dt_in = sem("dt_in")
        dt_exp = sem("dt_exp")
        a_ready = sem("a_ready")
        cs_pe = sem("cs_pe")
        cs_ready = sem("cs_ready")
        ws_ready = sem("ws_ready")
        trA, trB = sem("trA"), sem("trB")
        trA_out, trB_out = sem("trA_out"), sem("trB_out")
        xw_ready = sem("xw_ready")
        st_pe = sem("st_pe")
        st_ready = sem("st_ready")
        pm_pe, pm_out = sem("pm_pe"), sem("pm_out")
        s_ready = sem("s_ready")
        max_ready = sem("max_ready")
        exp_ready = sem("exp_ready")
        p_ready = sem("p_ready")
        pv_pe, pv_out = sem("pv_pe"), sem("pv_out")
        g_pe, cb_pe = sem("g_pe"), sem("cb_pe")
        gm_ready = sem("gm_ready")
        d_ready, d_back_ready = sem("d_ready"), sem("d_back_ready")
        ecum_ready = sem("ecum_ready")
        e_ready = sem("e_ready")
        w_ready, w_back_ready = sem("w_ready"), sem("w_back_ready")
        cdec_ready = sem("cdec_ready")
        xdt_ready = sem("xdt_ready")
        y_pe, y_out = sem("y_pe"), sem("y_out")
        gz_ready = sem("gz_ready")
        gsq_ready = sem("gsq_ready")
        gss_pe, gss_out = sem("gss_pe"), sem("gss_out")
        groot_ready = sem("groot_ready")
        gn_done = sem("gn_done")
        m_hi_ready, m_lo_ready = sem("m_hi_ready"), sem("m_lo_ready")
        o_pe = sem("o_pe")
        out_a, out_b = sem("out_a"), sem("out_b")

        def lat0(l, after_mixers=True):
            return CTX if l == DEPTH - 1 else 0

        def spans(l):
            return [(CTX, T)] if l == DEPTH - 1 else [(0, CTX), (CTX, T)]

        def bank_of(p, a, b):
            return flat[:, 1024 * p + 256 + a:1024 * p + 256 + b]

        def tr_bank(k):
            return 2 if k % 2 == 0 or k >= 5 else 0

        tile_base = [l * N_TILES for l in range(DEPTH)]
        up_base, down_base = [], []
        for l in range(DEPTH):
            n = tile_base[l] + N_FEAT + N_TOK + N_OUT
            ub, db = [], []
            for f in FF_BLOCKS:
                ub.append(n)
                db.append(n + 2 * f)
                n += 2 * f + KC
            up_base.append(ub)
            down_base.append(db)

        def pair_use(n):
            l, k = n // N_TILES, n % N_TILES
            return (l * (N_TILES - N_TOK) + (k if k < N_FEAT else k - N_TOK)) // 2 if not (
                N_FEAT <= k < N_FEAT + N_TOK) else (l * (N_TILES - N_TOK) + N_FEAT) // 2

        STEPS_AT = (3, 3, 2, 0)

        def part_base(l, part):
            return (l * N_MOD + part) * KC

        def mixer_events(l):
            fwd, bwd = list(range(TT)), [1, 0, 5, 4, 3, 2]
            chunks = list(range(TT)) if l < DEPTH - 1 else list(range(2, TT))
            states = []
            for k in range(TT - 1):
                states += [("state", 0, fwd[k], fwd[k + 1]), ("state", 1, bwd[k], bwd[k + 1])]
            ev = [("tr", "x", 0), ("tr", "x", 1), ("tr", "b", 0), ("cs",), ("pool", 0), ("pool", 1), ("tr", "q", 0)]
            ev += states[:4] + [("tr", "k", 0), ("tr", "k", 1)]
            states = states[4:]
            units = []
            for h in range(ATT_HEADS):
                if l < DEPTH - 1:
                    units.append((h, -1))
                units += [(h, t) for t in range(SEQ // P)]
            n_sp = len(spans(l))
            gates = []
            for ft in range(2):
                gates += [("gz", ft)] + [("gs", ft, k) for k in range(n_sp)]
            gates += [("gr",)] + [("gi", ft, a) for ft in range(2) for a in range(lat0(l), T, 256)]
            todo = list(chunks)
            last_c, two_buffers = None, None
            for u in range(len(units) + 3):
                if u < len(units):
                    if two_buffers is None and not states and not todo:
                        two_buffers = u
                    ev.append(("S", u, units[u]))
                if 2 <= u < len(units) + 2:
                    ev.append(("trP", u - 2, units[u - 2]))
                if u < len(units):
                    ev.append(("exp", u, units[u]))
                if u >= 3:
                    ev.append(("PV", u - 3, units[u - 3]))
                gate_now = not todo and last_c is None
                if last_c is not None:
                    ev.append(("ssd_y", last_c))
                    last_c = None
                if gate_now and gates and gates[0][0] != "gi":
                    ev.append(gates.pop(0))
                if todo and not states:
                    last_c = todo.pop(0)
                    ev.append(("ssd", last_c))
                for _ in range(2):
                    if states:
                        ev.append(states.pop(0))
                if gate_now and gates:
                    ev.append(gates.pop(0))
                if u < len(units) and units[u][1] == 1 and units[u][0] + 1 < ATT_HEADS:
                    ev.append(("tr", "q", units[u][0] + 1))
            ev += gates
            assert not todo and last_c is None and not states
            return ev, units, two_buffers

        def score_bank(u, two_buffers):
            return 4 if u >= two_buffers and (u - two_buffers) % 2 == 0 else 0

        block = stack.enter_context(nc.Block())

        @block.sync
        def _(sp):
            def vector_rows(l):
                for dst, n, src in (
                    (V_BMOD, 48, b_mod[l].rearrange("(r p) -> r p", p=P)), (V_N1, 8, norm1_w[l].rearrange("(r p) -> r p", p=P)),
                    (V_N2, 8, norm2_w[l].rearrange("(r p) -> r p", p=P)), (V_PS, 2, pool_scale[l].rearrange("(r p) -> r p", p=P)),
                    (V_CB, 4, conv_b[l].rearrange("(r p) -> r p", p=P)), (V_CW, 20, conv_w[l].rearrange("k (r p) -> (k r) p", p=P)),
                    (V_SN, 2, ssd_norm_w[l].rearrange("(r p) -> r p", p=P)),
                ):
                    sp.dma_start(vrows[l][dst:dst + n, :], src).then_inc(vrows_landed[l], 16)
                if l == 0:
                    sp.dma_start(vrows[0][V_C:V_C + 8, :], c[0].rearrange("(r p) -> r p", p=P)).then_inc(vrows_landed[0], 16)
                    sp.dma_start(vrows[0][V_C + 8:V_C + 16, :], c_ctx.rearrange("(r p) -> r p", p=P)).then_inc(vrows_landed[0], 16)

            def load_mod(l, part, kc, slot, used):
                if used is not None:
                    sp.wait_ge(mod_used, used)
                sp.dma_start(mod_ring[slot][:, :], w_mod[l, kc * P:(kc + 1) * P, bass.ds(part * D, D)]).then_inc(mod_landed[slot], 16)

            def load_tile(slot, need_lo, src, n_k, width):
                if need_lo is not None:
                    sp.wait_ge(lo_ready, need_lo)
                dst = raw[slot][:, 0:n_k * width].rearrange("p (k n) -> p k n", k=n_k)
                sp.dma_start(dst, src).then_inc(raw_landed[slot], 16)

            def cols(w, l, col, width=P, k0=0, n_k=KC):
                return w[l].rearrange("(k p) n -> p k n", p=P)[:, k0:k0 + n_k, bass.ds(col, width)]

            sp.dma_start(ident, table[:, 0:P]).then_inc(ident_landed, 16)
            vector_rows(0)
            for s in range(2 * KC):
                if s == 4:
                    sp.dma_start(tab[:, P:], table[:, P:]).then_inc(table_landed, 16)
                load_mod(0, s // KC, s % KC, s % 4, s - 3 if s >= 4 else None)
            vector_rows(1)
            for l in range(DEPTH):
                base = tile_base[l]
                for n in range(N_FEAT):
                    load_tile(n % 4, base + n - 3 if base + n >= 4 else None, cols(w_in, l, FEAT_COLS[n]), KC, P)
                    for s in range(STEPS_AT[n % 4]):
                        k = sum(STEPS_AT[:n % 4]) + s
                        part = 2 + n // 4
                        load_mod(l, part, k, k % 4, part_base(l, part) + k - 3)
                with sp.Fori(0, 2) as i:
                    nb = base + N_FEAT
                    for j in range(4):
                        col = OFF_TOK + 520 * i if j < 2 else OFF_TOK + 264 + 512 * i
                        width = 264 if j < 2 else 256
                        load_tile(j, i * 4 + (nb + j - 3), cols(w_in, l, col, width, 4 * (j % 2), 4), 4, width)
                        for s in range(STEPS_AT[j]):
                            k = sum(STEPS_AT[:j]) + s
                            load_mod(l, 4 + i, k, k % 4, i * KC + (part_base(l, 4) + k - 3))
                with sp.Fori(0, 2) as i:
                    nb = base + N_FEAT + N_TOK
                    for j in range(4):
                        load_tile(j, i * 4 + (nb + j - 3), cols(w_out, l, i * (4 * P) + j * P), KC, P)
                f0 = 0
                for b, nf in enumerate(FF_BLOCKS):
                    nb = up_base[l][b]

                    def up(i, with_mod, first):
                        for j in range(4):
                            load_tile(j, i * 4 + (nb + j - 3), cols((w1, w3)[j % 2], l, i * (2 * P) + (f0 + j // 2) * P), KC, P)
                            for s in range(STEPS_AT[j] if with_mod else 0):
                                k = sum(STEPS_AT[:j]) + s
                                load_mod(l + 1, i, k, k % 4, i * KC + (part_base(l + 1, 0) + k - 3))
                    if b == 0 and l < DEPTH - 1:
                        sp.wait_ge(y_pe, l * INCS["y_pe"] + TT)
                        with sp.Fori(0, 2) as i:
                            up(i, True, True)
                        with sp.Fori(2, nf // 2) as i:
                            up(i, False, False)
                    else:
                        with sp.Fori(0, nf // 2) as i:
                            up(i, False, False)
                    nb2 = down_base[l][b]
                    with sp.Fori(0, 2) as i:
                        for j in range(4):
                            load_tile(j, i * 4 + (nb2 + j - 3), cols(w2, l, i * (4 * P) + j * P, P, f0, nf), nf, P)
                    f0 += nf
            for t in range(SEQ // P):
                sp.wait_ge(out_a, t + 1)
                sp.wait_ge(out_b, t + 1)
                sp.dma_start(out[0, t * P:(t + 1) * P, :], x_out[:, t, :]).then_inc(out_stored, 16)
            sp.wait_ge(out_stored, 16 * (SEQ // P))

        @block.gpsimd
        def _(pool):
            own = OwnOrder(s_pool)

            def link(ins):
                pool.wait_ge(s_pool, own.mark(ins))

            pool.memset(mod_rows[:, :], 0.0).then_inc(zeroed, 1)
            pool.memset(eps[:, :], EPS).then_inc(zeroed, 1)
            for s in range(4):
                pool.memset(raw[s][:, D:WT], 0.0).then_inc(zeroed, 1)
            for l in range(DEPTH):
                pool.memset(pool_bd[l][:, :, :], 0.0).then_inc(zeroed, 1)

            def sum_squares(n, r0):
                for j in range(1, KC - 1):
                    pool.wait_ge(sq_ready, n * INCS["sq_ready"] + j + 1)
                    if j > 1:
                        pool.wait_ge(acc_ready, n * INCS["acc_ready"] + j - 1)
                    in0 = sq[:, 0, r0:T] if j == 1 else sq_acc[:, r0:T]
                    pool.tensor_tensor(sq_acc[:, r0:T], in0, sq[:, j % 2, r0:T], ALU.add).then_inc(acc_ready, 1)

            for l in range(DEPTH):
                r0 = lat0(l)
                sum_squares(2 * l, 0)
                pool.wait_ge(h_lo_ready, (2 * l) * INCS["h_lo_ready"] + KC)
                for ft in range(2):
                    for a, b in ((0, PC0), (PC0 + CTX, PL0), (PL0 + SEQ, PW)):
                        pool.memset(pool_u[:, ft, a:b], 0.0).then_inc(pads_zero, 1)
                pool.wait_ge(pads_zero, l * INCS["pads_zero"] + 6)
                pool.memset(c_T[64:P, 0, :], 0.0).then_inc(pads_zero, 1)
                pool.wait_ge(pads_zero, l * INCS["pads_zero"] + 7)
                pool.memset(c_T[0:64, 1, :], 0.0).then_inc(pads_zero, 1)
                lo = 0 if l < DEPTH - 1 else PL0 - PAD
                w0, w1_ = (PC0 if l < DEPTH - 1 else PL0), PL0 + SEQ
                pool.wait_ge(pads_zero, l * INCS["pads_zero"] + 8)
                for ft in range(2):
                    pool.wait_ge(pair_free[ft], pair_use(tile_base[l] + ft) + 1)
                    u = pool_u[:, ft, :]
                    link(pool.tensor_tensor(win_a[:, lo + 1:PW], u[:, lo:PW - 1], u[:, lo + 1:PW], ALU.add))
                    if ft == 0:
                        link(pool.tensor_tensor(win_b[64:P, lo + 2:PW - 1], win_a[64:P, lo + 1:PW - 2],
                                                win_a[64:P, lo + 3:PW], ALU.add))
                    else:
                        link(pool.tensor_tensor(win_b[:, lo + 2:PW - 1], win_a[:, lo + 1:PW - 2], win_a[:, lo + 3:PW], ALU.add))
                        link(pool.tensor_tensor(win_a[:, lo + 4:PW - 3], win_b[:, lo + 2:PW - 5], win_b[:, lo + 6:PW - 1], ALU.add))
                        link(pool.tensor_tensor(win_b[64:P, lo + 8:PW - 7], win_a[64:P, lo + 4:PW - 11],
                                                win_a[64:P, lo + 12:PW - 3], ALU.add))
                    pool.wait_ge(count_landed, 16 * (2 * l + ft + 1))
                    link(pool.tensor_tensor(win_a[0:64, w0:w1_], win_a[0:64, w0:w1_], inv_n[0:64, w0:w1_], ALU.mult))
                    pool.tensor_tensor(win_a[64:P, w0:w1_], win_b[64:P, w0:w1_], inv_n[64:P, w0:w1_], ALU.mult).then_inc(count_used, 1)
                    pool.wait_ge(count_used, l * INCS["count_used"] + ft + 1)
                    pool.tensor_tensor(u[:, w0:w1_], win_a[:, w0:w1_], u[:, w0:w1_], ALU.subtract).then_inc(pooled_ready, 1)
                    pool.wait_ge(pooled_ready, l * INCS["pooled_ready"] + ft + 1)
                for blk in range(3):
                    pool.wait_ge(qkn_ready, l * INCS["qkn_ready"] + blk + 1)
                    if blk:
                        pool.wait_ge(qk_ready, l * INCS["qk_ready"] + blk)
                    xv = qk[:, blk, 2:TT, :].rearrange("p t n -> p (t n)").rearrange("p (g h e) -> p g h e", h=2, e=32)
                    sv = rope_s.rearrange("p (g h e) -> p g h e", h=2, e=32)
                    tv = rope_t[:, :].rearrange("p (g h e) -> p g h e", h=2, e=32)
                    for half in range(2):
                        pool.tensor_tensor(tv[:, :, half, :], xv[:, :, 1 - half, :], sv[:, :, half, :], ALU.mult)\
                            .then_inc(rope_s_ready, 1)
                ev, units, two_buffers = mixer_events(l)
                n_st = n_y = 0
                for e in ev:
                    if e[0] == "state":
                        _, d, cc, _n = e
                        if n_st == 0:
                            pool.wait_ge(ws_ready, l * INCS["ws_ready"] + 1)
                            pool.wait_ge(trA_out, l * INCS["trA_out"] + 3)
                            pool.wait_ge(trB_out, l * INCS["trB_out"] + 3)
                        if n_st >= 2:
                            pool.wait_ge(st_pe, l * INCS["st_pe"] + n_st - 1)
                        pool.tensor_tensor(x_w[:, n_st % 2, :].rearrange("p (h q) -> p h q", h=HEADS),
                                           x_tok[:, cc, :].rearrange("p (h q) -> p h q", h=HEADS),
                                           w_state[:, d, cc, :].unsqueeze(2).to_broadcast([P, HEADS, HD_SSD]), ALU.mult)\
                            .then_inc(xw_ready, 1)
                        n_st += 1
                    elif e[0] == "ssd":
                        cc = e[1]
                        if n_y:
                            pool.wait_ge(y_pe, l * INCS["y_pe"] + n_y)
                        for d in range(DIRS):
                            pool.tensor_tensor(x_dt[:, d, :].rearrange("p (h q) -> p h q", h=HEADS),
                                               x_tok[:, cc, :].rearrange("p (h q) -> p h q", h=HEADS),
                                               dts[:, cc, 4 * d:4 * d + 4].unsqueeze(2).to_broadcast([P, HEADS, HD_SSD]), ALU.mult)\
                                .then_inc(xdt_ready, 1)
                        for d in range(DIRS):
                            pool.wait_ge(ecum_ready, l * INCS["ecum_ready"] + 2 * n_y + d + 1)
                            pool.tensor_tensor(e_cum[:, d, :, :].rearrange("p (g r) s -> p g r s", r=2),
                                               e_cum[:, d, :, :].rearrange("p (g r) s -> p g r s", r=2),
                                               c_T[:, :, cc * P:(cc + 1) * P].unsqueeze(2).to_broadcast([P, 2, 2, P]), ALU.mult)\
                                .then_inc(cdec_ready, 1)
                        pool.wait_ge(e_ready, l * INCS["e_ready"] + 2 * n_y + 2)
                        pool.wait_ge(gm_ready, l * INCS["gm_ready"] + 2 * n_y + 2)
                        v = e_in[:, 1, :, :].rearrange("p (g r) s -> p g r s", r=2)
                        pool.tensor_tensor(v, v, g_mask[:, 1, :, :].unsqueeze(2).to_broadcast([P, 2, 2, P]), ALU.mult)\
                            .then_inc(w_back_ready, 1)
                        n_y += 1
                sum_squares(2 * l + 1, r0)

        @block.scalar
        def _(act):
            own = OwnOrder(s_act)

            def link(ins):
                act.wait_ge(s_act, own.mark(ins))

            def bcast(dst, src, n=P):
                act.dma_start(dst, src.partition_broadcast(n)).then_inc(small_landed, 16)

            n_small = 0
            for t in range(TT):
                src = ctx[0, t * P:(t + 1) * P, :] if t < CTX // P else x[0, (t - CTX // P) * P:(t - CTX // P + 1) * P, :]
                act.dma_start(x_in[:, t, :], src).then_inc(x_landed[t], 16)
            act.wait_ge(zeroed, 6 + DEPTH)
            for l in range(DEPTH):
                bcast(dt_b[l][:, :], dt_bias[l].rearrange("d h -> (d h)"))
                bcast(neg_a[l][:, :], a_log[l].rearrange("d h -> (d h)"))
                bcast(qk_w[l][:, 0, :], q_norm_w[l])
                bcast(qk_w[l][:, 1, :], k_norm_w[l])
                bcast(skip2[l][:, :], d_skip[l].rearrange("d h -> (d h)"))
                for half in range(2):
                    for ft in range(2):
                        act.dma_start(pool_bd[l][64 * half:64 * half + 64, ft, 64 * half:64 * half + 64],
                                      pool_w[l, 2 * ft + half]).then_inc(small_landed, 16)
                n_small += 9

            def vectors(l):
                act.wait_ge(vec_T, l + 1)
                n = N_VEC[l]
                act.activation(vecs[l][:, 0:n], banks[:, 4 + l, 0:n], ACT.Copy).then_inc(vec_ready, 1)

            def split_hi(n, i4=0):
                act.wait_ge(raw_landed[n % 4], i4 * 4 + 16 * (n // 4 + 1))
                if n >= 2:
                    act.wait_ge(tile_done, i4 + (n - 1))
                act.activation(w_hi[n % 2][:, :], raw[n % 4][:, :], ACT.Copy).then_inc(hi_ready, 1)

            def mod_rows_out(q):
                act.wait_ge(mod_used, KC * (q + 1))
                if q:
                    act.wait_ge(rows_T, q)
                for g in range(4):
                    act.activation(mod_rows[32 * g:32 * g + 2, :], banks[32 * g:32 * g + 2, 7, 0:256], ACT.Copy).then_inc(rows_ready, 1)

            def square_chunk(n, j, r0):
                if j >= 2:
                    act.wait_ge(acc_ready, n * INCS["acc_ready"] + max(1, j - 2))
                act.activation(sq[:, j % 2, r0:T], x_res[:, j, r0:T], ACT.Square).then_inc(sq_ready, 1)

            def norm(l, which, sp_, next_tile):
                n = 2 * l + which
                r0 = sp_[0][0]
                split_hi(next_tile + 1)
                act.wait_ge(ss_ready, n * INCS["ss_ready"] + 1)
                act.activation(rstd[:, r0:T], bank_of(3, r0, T), ACT.Sqrt, bias=eps[:, 0:1], scale=1.0 / D).then_inc(root_ready, 1)
                act.wait_ge(gain_ready, n + 1)
                for j in range(KC):
                    act.wait_ge(t_ready, n * INCS["t_ready"] + j + 1)
                    for a, b in sp_:
                        g = 0 if a == CTX else 1
                        m = own.mark(act.activation(nrm[:, j % 2, a:b], nrm[:, j % 2, a:b], ACT.Identity,
                                                    bias=mods[l][:, 3 * which, g, j:j + 1], scale=gain[l][:, which, g, j:j + 1]))
                    act.wait_ge(s_act, m)
                    act.activation(h_hi[:, j, r0:T], nrm[:, j % 2, r0:T], ACT.Copy).then_inc(h_hi_ready, 1)

            act.wait_ge(zeroed, 6 + DEPTH)
            vectors(0)
            act.wait_ge(vec_ready, 1)
            act.activation(cond[:, :, :].rearrange("p c k -> p (c k)"), vecs[0][:, V_C:V_C + 16], ACT.Silu).then_inc(cond_ready, 1)
            for t in range(TT):
                act.wait_ge(xT_pe, 2 * t + 1)
                act.activation(x_res[:, 0:4, t * P:(t + 1) * P], banks[:, 2 * (t % 2), :].rearrange("p (k n) -> p k n", k=4),
                               ACT.Copy).then_inc(xT_a, 1)
                if t == 3:
                    mod_rows_out(0)
            act.wait_ge(xT_a, TT)
            act.wait_ge(xT_b, TT)
            for j in range(KC):
                square_chunk(0, j, 0)
            mod_rows_out(1)
            vectors(1)
            act.wait_ge(small_landed, 16 * n_small)
            for l in range(DEPTH):
                act.activation(neg_a[l][:, :], neg_a[l][:, :], ACT.Exp).then_inc(small_act, 1)
            split_hi(0)
            for l in range(DEPTH):
                base = tile_base[l]
                sp_ = spans(l)
                r0 = lat0(l)
                norm(l, 0, [(0, CTX), (CTX, T)], base)
                act.wait_ge(h_lo_ready, (2 * l) * INCS["h_lo_ready"] + KC)
                act.dma_start(inv_n[:, :], count[0]).then_inc(count_landed, 16)

                def silu_xbc(k):
                    act.wait_ge(pair_free[k % 2], pair_use(base + 2 + k) + 1)
                    acc = conv_acc[:, k % 2, :]
                    if k < 2:
                        act.activation(x_T[:, k, :], acc, ACT.Silu).then_inc(xbc_ready, 1)
                    elif k == 2:
                        act.activation(b_T[:, :], acc, ACT.Silu).then_inc(xbc_ready, 1)
                    else:
                        act.activation(c_T[0:64, 0, :], conv_acc[0:64, k % 2, :], ACT.Silu).then_inc(xbc_ready, 1)
                        act.activation(c_T[64:P, 1, :], conv_acc[64:P, k % 2, :], ACT.Silu).then_inc(xbc_ready, 1)

                for n in range(N_FEAT):
                    N = base + n
                    if n:
                        split_hi(N + 1)
                    if n < 2:
                        act.wait_ge(tile_done, N + 1)
                        if l < DEPTH - 1:
                            act.activation(pool_u[:, n, PC0:PC0 + CTX], bank_of(n % 2, 0, CTX), ACT.Copy)
                        act.activation(pool_u[:, n, PL0:PL0 + SEQ], bank_of(n % 2, CTX, T), ACT.Copy).then_inc(pair_free[n % 2], 1)
                    if 3 <= n <= 6:
                        silu_xbc(n - 3)
                    if n == 4:
                        act.wait_ge(count_used, l * INCS["count_used"] + 1)
                        act.dma_start(inv_n[:, :], count[1]).then_inc(count_landed, 16)
                    if n % 4 == 3:
                        mod_rows_out(l * N_MOD + 2 + n // 4)
                    if n >= 6:
                        act.wait_ge(tile_done, N + 1)
                        act.activation(silu_z[:, n - 6, r0:T], bank_of(n % 2, r0, T), ACT.Silu).then_inc(pair_free[n % 2], 1)
                for n in range(N_TOK):
                    N = base + N_FEAT + n
                    split_hi(N + 1)
                    b = n // 2
                    if n % 4 == 3:
                        mod_rows_out(l * N_MOD + 4 + n // 4)
                    if n % 2 == 0:
                        if 1 <= b:
                            act.wait_ge(qkss_ready, l * INCS["qkss_ready"] + b)
                            act.activation(qk_rt[:, b - 1, :], qk_ss[:, b - 1, :], ACT.Sqrt, bias=eps[:, 0:1],
                                           scale=1.0 / HEAD_DIM).then_inc(qkrt_ready, 1)
                        continue
                    for t in range(TT):
                        if t < TT - 1:
                            act.wait_ge(tok_ready, (l * 4 + b) * (TT - 1) + t + 1)
                        else:
                            act.wait_ge(tile_done, N + 1)
                        off = 8 if b == 0 else 0
                        if b == 0:
                            act.activation(dt_raw[:, t, :], banks[:, t, 0:8], ACT.Copy)
                        dst = qk[:, b, t, :] if b < 3 else v_tok[:, t, :]
                        act.activation(dst, banks[:, t, off:off + 256], ACT.Copy).then_inc(tok_free, 1)
                    if b < 3:
                        act.wait_ge(tok_free, (l * 4 + b + 1) * TT)
                        if b:
                            act.wait_ge(qkss_ready, l * INCS["qkss_ready"] + b)
                        act.activation(qk_sq[:, :, :].rearrange("p a n -> p (a n)"), qk[:, b, :, :].rearrange("p t n -> p (t n)"),
                                       ACT.Square).then_inc(qksq_ready, 1)
                    if b == 1:
                        act.wait_ge(dt_in, l * INCS["dt_in"] + 1)
                        act.activation(dt_n[:, :, :], dt_n[:, :, :], ACT.Exp).then_inc(dt_exp, 1)
                        act.wait_ge(dt_exp, l * INCS["dt_exp"] + 1)
                        act.activation(dt_n[:, :, :], dt_n[:, :, :], ACT.Ln, bias=ones[:, 0:1]).then_inc(dt_exp, 1)

                ev, units, two_buffers = mixer_events(l)
                nA = n_pv = n_y = n_gs = 0
                job_of = {}
                for e in ev:
                    if e[0] == "tr":
                        act.wait_ge(trA, l * INCS["trA"] + nA + 1)
                        src = banks[:, tr_bank(nA), :]
                        if e[1] == "x":
                            act.activation(x_tok[:, 0:4, e[2] * P:(e[2] + 1) * P], src.rearrange("p (t n) -> p t n", t=4), ACT.Copy).then_inc(trA_out, 1)
                        elif e[1] == "b":
                            act.activation(b_tok[:, 0:4, :], src.rearrange("p (t n) -> p t n", t=4), ACT.Copy).then_inc(trA_out, 1)
                        elif e[1] == "k":
                            act.activation(k_T[:, e[2], 0:512], src, ACT.Copy).then_inc(trA_out, 1)
                        else:
                            act.activation(q_T[:, e[2] % 2, CTX:T], src, ACT.Copy, scale=float(HEAD_DIM) ** -0.5).then_inc(trA_out, 1)
                        nA += 1
                    elif e[0] == "cs":
                        act.wait_ge(cs_pe, l * INCS["cs_pe"] + 1)
                        act.activation(decay[:, :, :, :].rearrange("p d c h -> p (d c h)"), banks[:, 7, 48:96], ACT.Exp).then_inc(cs_ready, 1)
                        act.activation(decay_all[:, :, :].rearrange("p c h -> p (c h)"), banks[:, 7, 96:144], ACT.Exp).then_inc(cs_ready, 1)
                        act.activation(cs_tok[:, :, :, :].rearrange("p d c h -> p (d c h)"), banks[:, 7, 0:48], ACT.Copy).then_inc(cs_ready, 1)
                    elif e[0] == "pool":
                        act.wait_ge(pm_pe, l * INCS["pm_pe"] + 2)
                        act.activation(mix[:, e[1], r0:T], bank_of(2 + e[1], r0, T),
                                       ACT.Copy, scale=vecs[l][:, V_PS + e[1]:V_PS + e[1] + 1]).then_inc(pm_out, 1)
                    elif e[0] == "exp":
                        u, (h, t) = e[1], e[2]
                        act.wait_ge(max_ready, l * INCS["max_ready"] + u + 1)
                        if u >= 3:
                            act.wait_ge(trA, l * INCS["trA"] + job_of[u - 3] + 1)
                        sb = score_bank(u, two_buffers)
                        if t < 0:
                            act.activation(probs[:, u % 3, 0:256], banks[:, sb, 0:256], ACT.Exp, bias=neg_max[:, u % 2, 0:1],
                                           accum_out=p_sum[:, u % 2, 0:1])
                            act.activation(probs[:, u % 3, 256:512], banks[:, sb, 256:512], ACT.Exp, bias=neg_max[:, u % 2, 1:2],
                                           accum_out=p_sum[:, u % 2, 1:2]).then_inc(exp_ready, 1)
                        else:
                            act.activation(probs[:, u % 3, :], flat[:, 512 * sb:512 * sb + T], ACT.Exp, bias=neg_max[:, u % 2, 0:1],
                                           accum_out=p_sum[:, u % 2, 0:1]).then_inc(exp_ready, 1)
                    elif e[0] == "trP":
                        u, (h, t) = e[1], e[2]
                        job_of[u] = nA
                        act.wait_ge(trA, l * INCS["trA"] + nA + 1)
                        if u >= 2:
                            act.wait_ge(pv_pe, l * INCS["pv_pe"] + u - 1)
                        if t < 0:
                            act.activation(p_T[:, u % 2, 0:4, :].rearrange("p (k q) n -> p q k n", q=2),
                                           banks[:, 2, :].rearrange("p (q k n) -> p q k n", q=2, k=2), ACT.Copy).then_inc(trA_out, 1)
                        else:
                            act.activation(p_T[:, u % 2, 0:4, :], banks[:, 2, :].rearrange("p (k n) -> p k n", k=4), ACT.Copy).then_inc(trA_out, 1)
                        nA += 1
                    elif e[0] == "PV":
                        u, (h, t) = e[1], e[2]
                        if t < 0 or t == SEQ // P - 1:
                            a, b = (0, CTX) if t < 0 else (CTX, T)
                            act.wait_ge(pv_pe, l * INCS["pv_pe"] + u + 1)
                            act.activation(mix[:, 4 + h, a:b], banks[:, 7, 0:b - a], ACT.Copy).then_inc(pv_out, 1)
                            n_pv += 1
                    elif e[0] == "ssd":
                        cc = e[1]
                        if n_y:
                            act.wait_ge(y_pe, l * INCS["y_pe"] + n_y)
                        for d in range(DIRS):
                            act.wait_ge(cb_pe, l * INCS["cb_pe"] + 2 * n_y + d + 1)
                            act.activation(e_cum[:, d, :, :].rearrange("p h s -> p (h s)"), banks[:, 5 - d, :], ACT.Exp).then_inc(ecum_ready, 1)
                        for h in range(HEADS):
                            ins = act.activation(e_in[:, 1, h, :], banks[:, 4, h * P:(h + 1) * P], ACT.Relu,
                                                 bias=cs_tok[:, 1, cc, h:h + 1], scale=-1.0)
                        ins.then_inc(d_back_ready, 1)
                        act.wait_ge(d_ready, l * INCS["d_ready"] + n_y + 1)
                        act.activation(e_in[:, 0, :, :], e_in[:, 0, :, :], ACT.Exp).then_inc(e_ready, 1)
                        act.wait_ge(d_back_ready, l * INCS["d_back_ready"] + n_y + 1)
                        act.activation(e_in[:, 1, :, :], e_in[:, 1, :, :], ACT.Exp, scale=-1.0).then_inc(e_ready, 1)
                        n_y += 1
                    elif e[0] == "gz":
                        act.wait_ge(gz_ready, l * INCS["gz_ready"] + e[1] + 1)
                        if e[1]:
                            act.wait_ge(gss_pe, l * INCS["gss_pe"] + len(sp_))
                        act.activation(gn_sq[:, r0:T], mix[:, 2 + e[1], r0:T], ACT.Square).then_inc(gsq_ready, 1)
                    elif e[0] == "gs":
                        a, b = sp_[e[2]]
                        act.wait_ge(gss_pe, l * INCS["gss_pe"] + n_gs + 1)
                        act.activation(gn_r[:, e[1], a:b], banks[:, 6, 0:b - a], ACT.Copy).then_inc(gss_out, 1)
                        n_gs += 1
                    elif e[0] == "gr":
                        act.wait_ge(gss_out, l * INCS["gss_out"] + n_gs)
                        act.activation(gn_r[:, :, r0:T], gn_r[:, :, r0:T], ACT.Sqrt, bias=eps[:, 0:1], scale=1.0 / P).then_inc(groot_ready, 1)
                act.wait_ge(gn_done, l * INCS["gn_done"] + 2 * (T - r0) // 256)
                act.wait_ge(pv_out, l * INCS["pv_out"] + n_pv)
                for j in range(KC):
                    act.activation(h_hi[:, j, r0:T], mix[:, j, r0:T], ACT.Copy).then_inc(m_hi_ready, 1)

                for n in range(N_OUT):
                    split_hi(base + N_FEAT + N_TOK + n + 1)
                    act.wait_ge(pair_free[n % 2], pair_use(base + N_FEAT + N_TOK + n) + 1)
                    square_chunk(2 * l + 1, n, r0)
                norm(l, 1, sp_, up_base[l][0])
                for b, nf in enumerate(FF_BLOCKS):
                    nb = up_base[l][b]
                    gb = (l * sum(FF_BLOCKS) + sum(FF_BLOCKS[:b]))

                    def up(i, first=False, mod_part=None):
                        for j in range(4):
                            if not first or j:
                                split_hi(nb + j + 1, i * 4)
                            if j == 3 and mod_part is not None:
                                mod_rows_out(mod_part)
                            m = pair_use(nb + j)
                            if j % 2 == 0:
                                act.wait_ge(tile_done, i * 4 + (nb + j + 1))
                                act.activation(silu_a[:, r0:T], bank_of(0, r0, T), ACT.Silu).then_inc(pair_free[0], 1)
                            else:
                                f = j // 2
                                act.wait_ge(pair_free[1], i * 2 + (m + 1))
                                act.activation(g_hi[:, bass.ds(i * (2 * T) + f * T + r0, T - r0)],
                                               g_f[:, f, r0:T], ACT.Copy).then_inc(g_hi_ready, 1)
                    at = 0
                    if b == 0:
                        up(0, True, (l + 1) * N_MOD if l < DEPTH - 1 else None)
                        at = 1
                        if l < DEPTH - 1:
                            up(1, False, (l + 1) * N_MOD + 1)
                            at = 2
                    with act.Fori(at, nf // 2) as i:
                        up(i)
                    last = b == len(FF_BLOCKS) - 1
                    for n in range(KC):
                        N = down_base[l][b] + n
                        if N + 1 < DEPTH * N_TILES:
                            split_hi(N + 1)
                        if last and l < DEPTH - 1:
                            act.wait_ge(pair_free[n % 2], pair_use(N) + 1)
                            square_chunk(2 * l + 2, n, 0)
            for t in range(SEQ // P):
                act.wait_ge(o_pe, 2 * t + 1)
                act.activation(x_out[:, t, 0:512], banks[:, 2 * (t % 2), :], ACT.Copy).then_inc(out_a, 1)

        @block.vector
        def _(dve):
            own = OwnOrder(s_dve)

            def link(ins):
                dve.wait_ge(s_dve, own.mark(ins))

            def as_f32(ap):
                return ap.bitcast(F32)

            def split_lo(n, i4=0):
                dve.wait_ge(hi_ready, i4 + (n + 1))
                dve.tensor_tensor(w_lo[n % 2][:, :], raw[n % 4][:, :], as_f32(w_hi[n % 2][:, :]), ALU.subtract).then_inc(lo_ready, 1)

            def mod_bias(l, part):
                q = l * N_MOD + part
                dve.wait_ge(rows_T, q + 1)
                for t in range(2):
                    rows = banks[:, 6, P * t:P * t + P].rearrange("p (g r) -> p r g", g=4)[:, 0:2, :]
                    v0 = V_BMOD + KC * part + t
                    bias = vecs[l][:, v0:v0 + 7:2].unsqueeze(1).to_broadcast([P, 2, 4])
                    dve.tensor_tensor(mods[l][:, part, :, t:KC:2], rows, bias, ALU.add).then_inc(mods_ready, 1)

            def make_gain(l, which):
                dve.wait_ge(mods_ready, 2 * (l * N_MOD + 2 + 3 * which))
                v0 = (V_N1, V_N2)[which]
                dve.scalar_tensor_tensor(gain[l][:, which, :, :], mods[l][:, 1 + 3 * which, :, :], 1.0,
                                         vecs[l][:, v0:v0 + KC].unsqueeze(1).to_broadcast([P, 2, KC]),
                                         ALU.add, ALU.mult).then_inc(gain_ready, 1)

            def norm(l, which, sp_, next_tile):
                n = 2 * l + which
                r0 = sp_[0][0]
                split_lo(next_tile + 1)
                dve.wait_ge(root_ready, n * INCS["root_ready"] + 1)
                dve.reciprocal(rstd[:, r0:T], rstd[:, r0:T]).then_inc(rstd_ready, 1)
                dve.wait_ge(rstd_ready, n * INCS["rstd_ready"] + 1)

                def low(j):
                    dve.wait_ge(h_hi_ready, n * INCS["h_hi_ready"] + j + 1)
                    dve.tensor_tensor(h_lo[:, j, r0:T], nrm[:, j % 2, r0:T], as_f32(h_hi[:, j, r0:T]), ALU.subtract)\
                        .then_inc(h_lo_ready, 1)
                for j in range(KC):
                    if j >= 2:
                        low(j - 2)
                        dve.wait_ge(h_lo_ready, n * KC + j - 1)
                    dve.tensor_tensor(nrm[:, j % 2, r0:T], x_res[:, j, r0:T], rstd[:, r0:T], ALU.mult).then_inc(t_ready, 1)
                low(KC - 2)
                low(KC - 1)

            def gated_add(l, part, j, n, sp_):
                dve.wait_ge(tile_done, n + 1)
                for k, (a, b) in enumerate(sp_):
                    g = 0 if a == CTX else 1
                    ins = dve.scalar_tensor_tensor(x_res[:, j, a:b], bank_of(n % 2, a, b), mods[l][:, part, g, j:j + 1],
                                                   x_res[:, j, a:b], ALU.mult, ALU.add)
                    if k == len(sp_) - 1:
                        ins.then_inc(pair_free[n % 2], 1)

            dve.wait_ge(small_landed, 16 * 9 * DEPTH)
            for l in range(DEPTH):
                for half in range(2):
                    rows = slice(64 * half, 64 * half + 64)
                    dve.tensor_tensor(skip[l][rows, :], skip2[l][rows, half:HEADS:2], skip2[l][rows, HEADS + half:2 * HEADS:2],
                                      ALU.add).then_inc(small_ready, 1)
            for t in range(TT):
                dve.wait_ge(xT_pe, 2 * t + 2)
                dve.tensor_copy(x_res[:, 4:8, t * P:(t + 1) * P], banks[:, 2 * (t % 2) + 1, :].rearrange("p (k n) -> p k n", k=4))\
                    .then_inc(xT_b, 1)
            dve.wait_ge(vec_ready, 1)
            mod_bias(0, 0)
            mod_bias(0, 1)
            make_gain(0, 0)
            dve.wait_ge(small_act, DEPTH)
            for l in range(DEPTH):
                dve.tensor_scalar(neg_a[l][:, :], neg_a[l][:, :], -1.0, None, ALU.mult).then_inc(small_ready, 1)
            split_lo(0)

            for l in range(DEPTH):
                base = tile_base[l]
                sp_ = spans(l)
                r0 = lat0(l)
                norm(l, 0, [(0, CTX), (CTX, T)], base)

                def conv(k):
                    N = base + 2 + k
                    dve.wait_ge(tile_done, N + 1)
                    if k >= 2:
                        dve.wait_ge(xbc_ready, l * INCS["xbc_ready"] + k - 1)
                    acc = conv_acc[:, k % 2, :]
                    streams = [(0, CTX), (CTX, T)]

                    def w(tap):
                        c0 = V_CW + 4 * tap + k
                        return vecs[l][:, c0:c0 + 1]
                    marks = []
                    for a, b in streams:
                        marks.append(own.mark(dve.tensor_scalar(acc[:, a:b], bank_of(N % 2, a, b), w(2),
                                                                vecs[l][:, V_CB + k:V_CB + k + 1], ALU.mult, ALU.add)))
                    for tap in (0, 1, 3, 4):
                        s = tap - 2
                        for q, (a, b) in enumerate(streams):
                            lo, hi = max(a, a - s), min(b, b - s)
                            dve.wait_ge(s_dve, marks[q])
                            ins = dve.scalar_tensor_tensor(acc[:, lo:hi], bank_of(N % 2, lo + s, hi + s), w(tap),
                                                           acc[:, lo:hi], ALU.mult, ALU.add)
                            if tap == 4 and q == 1:
                                ins.then_inc(pair_free[N % 2], 1)
                            else:
                                marks[q] = own.mark(ins)

                for n in range(N_FEAT):
                    if n:
                        split_lo(base + n + 1)
                    if 2 <= n < 6:
                        conv(n - 2)
                    if n == 4:
                        mod_bias(l, 2)

                def reduce_heads(b):
                    dve.wait_ge(qksq_ready, l * INCS["qksq_ready"] + b + 1)
                    dve.tensor_reduce(qk_ss[:, b, :], qk_sq[:, :, :], AX_X, ALU.add).then_inc(qkss_ready, 1)

                def scale_heads(b):
                    dve.wait_ge(qkrt_ready, l * INCS["qkrt_ready"] + b + 1)
                    link(dve.reciprocal(qk_rt[:, b, :], qk_rt[:, b, :]))
                    for t in range(TT):
                        for h in range(2):
                            v = qk[:, b, t, P * h:P * h + P]
                            ins = dve.scalar_tensor_tensor(v, v, qk_rt[:, b, 2 * t + h:2 * t + h + 1], qk_w[l][:, b // 2, :],
                                                           ALU.mult, ALU.mult)
                    ins.then_inc(qkn_ready, 1)

                def rotate(b):
                    dve.wait_ge(rope_s_ready, l * INCS["rope_s_ready"] + 2 * b + 2)
                    v = qk[:, b, 2:TT, :].rearrange("p t n -> p (t n)")
                    link(dve.tensor_tensor(v, v, rope_c, ALU.mult))
                    dve.tensor_tensor(v, v, rope_t[:, :], ALU.add).then_inc(qk_ready, 1)

                for n in range(N_TOK):
                    split_lo(base + N_FEAT + n + 1)
                    if n == 0:
                        mod_bias(l, 3)
                    if n == 4:
                        mod_bias(l, 4)
                        make_gain(l, 1)
                    if n == 2:
                        dve.wait_ge(tok_free, (4 * l + 1) * TT)
                        link(dve.tensor_tensor(dt_raw[:, :, :], dt_raw[:, :, :],
                                               dt_b[l][:, :].unsqueeze(1).to_broadcast([P, TT, N_DT]), ALU.add))
                        link(dve.tensor_scalar(dt_m[:, :, :], dt_raw[:, :, :], 0.0, None, ALU.max))
                        link(dve.tensor_scalar(dt_n[:, :, :], dt_raw[:, :, :], 0.0, None, ALU.min))
                        dve.tensor_tensor(dt_n[:, :, :], dt_n[:, :, :], dt_m[:, :, :], ALU.subtract).then_inc(dt_in, 1)
                    if n == 5:
                        dve.wait_ge(dt_exp, l * INCS["dt_exp"] + 2)
                        link(dve.tensor_tensor(dts[:, :, :], dt_m[:, :, :], dt_n[:, :, :], ALU.add))
                        dve.tensor_tensor(a_tok[:, :, :], dts[:, :, :], neg_a[l][:, :].unsqueeze(1).to_broadcast([P, TT, N_DT]),
                                          ALU.mult).then_inc(a_ready, 1)
                    if n >= 2 and n % 2 == 0:
                        reduce_heads(n // 2 - 1)
                    if n >= 3 and n % 2 == 1:
                        scale_heads((n - 3) // 2)
                    if n >= 4 and n % 2 == 0:
                        rotate((n - 4) // 2)
                mod_bias(l, 5)

                ev, units, two_buffers = mixer_events(l)
                nA = nB = n_st = n_y = n_pv = 0
                scaled = -1

                def scale_probs(u, t):
                    dve.wait_ge(exp_ready, l * INCS["exp_ready"] + u + 1)
                    if t < 0:
                        link(dve.reciprocal(p_inv[:, u % 2, 0:2], p_sum[:, u % 2, 0:2]))
                        for q in range(2):
                            v = probs[:, u % 3, 256 * q:256 * q + 256]
                            ins = dve.tensor_scalar(v, v, p_inv[:, u % 2, q:q + 1], None, ALU.mult)
                        ins.then_inc(p_ready, 1)
                    else:
                        link(dve.reciprocal(p_inv[:, u % 2, 0:1], p_sum[:, u % 2, 0:1]))
                        v = probs[:, u % 3, :]
                        dve.tensor_scalar(v, v, p_inv[:, u % 2, 0:1], None, ALU.mult).then_inc(p_ready, 1)

                def y_evac(cc, k):
                    dve.wait_ge(y_pe, l * INCS["y_pe"] + k + 1)
                    for ft in range(2):
                        dve.scalar_tensor_tensor(mix[:, 2 + ft, cc * P:(cc + 1) * P], x_T[:, ft, cc * P:(cc + 1) * P],
                                                 skip[l][:, ft:ft + 1], banks[:, 6, ft * P:(ft + 1) * P],
                                                 ALU.mult, ALU.add).then_inc(y_out, 1)

                for e in ev:
                    if e[0] == "tr":
                        if e[1] != "q" or l < DEPTH - 1:
                            if e[1:] == ("k", 0):
                                rotate(2)
                            dve.wait_ge(trB, l * INCS["trB"] + nB + 1)
                            src = banks[:, tr_bank(nA) + 1, 0:256]
                            if e[1] == "x":
                                ins = dve.tensor_copy(x_tok[:, 4:6, e[2] * P:(e[2] + 1) * P], src.rearrange("p (t n) -> p t n", t=2))
                            elif e[1] == "b":
                                ins = dve.tensor_copy(b_tok[:, 4:6, :], src.rearrange("p (t n) -> p t n", t=2))
                            elif e[1] == "k":
                                ins = dve.tensor_copy(k_T[:, e[2], 512:T], src)
                            else:
                                ins = dve.tensor_scalar(q_T[:, e[2] % 2, 0:CTX], src, float(HEAD_DIM) ** -0.5, None, ALU.mult)
                            ins.then_inc(trB_out, 1)
                            nB += 1
                        nA += 1
                    elif e[0] == "cs":
                        dve.wait_ge(cs_ready, l * INCS["cs_ready"] + 1)
                        dve.tensor_tensor(w_state[:, :, :, :], decay[:, :, :, :],
                                          dts[:, :, :].rearrange("p c (d h) -> p d c h", d=DIRS), ALU.mult).then_inc(ws_ready, 1)
                        dve.wait_ge(cs_ready, l * INCS["cs_ready"] + 3)
                    elif e[0] == "state":
                        _, d, cc, nxt = e
                        first = cc == (0, 1)[d]
                        dst = h_prev[:, d, nxt, :].rearrange("p (h q) -> p h q", h=HEADS)
                        if n_st == 0:
                            dve.wait_ge(mod_used, KC * (l * N_MOD + N_MOD))
                        if first:
                            dve.wait_ge(st_pe, l * INCS["st_pe"] + n_st + 1)
                            dve.tensor_copy(h_prev[:, d, nxt, :], banks[:, 4 + n_st % 2, 0:256]).then_inc(st_ready, 1)
                        else:
                            dve.wait_ge(st_ready, l * INCS["st_ready"] + n_st - 1)
                            link(dve.tensor_tensor(dst, h_prev[:, d, cc, :].rearrange("p (h q) -> p h q", h=HEADS),
                                                   decay_all[:, cc, 4 * d:4 * d + 4].unsqueeze(2).to_broadcast([P, HEADS, HD_SSD]), ALU.mult))
                            dve.wait_ge(st_pe, l * INCS["st_pe"] + n_st + 1)
                            dve.tensor_tensor(h_prev[:, d, nxt, :], h_prev[:, d, nxt, :], banks[:, 4 + n_st % 2, 0:256], ALU.add)\
                                .then_inc(st_ready, 1)
                        n_st += 1
                    elif e[0] == "S":
                        u, (h, t) = e[1], e[2]
                        if u:
                            scale_probs(u - 1, units[u - 1][1])
                            scaled = u - 1
                        dve.wait_ge(s_ready, l * INCS["s_ready"] + u + 1)
                        sb = score_bank(u, two_buffers)
                        if t < 0:
                            dve.tensor_reduce(neg_max[:, u % 2, 0:2], banks[:, sb, :].rearrange("p (q n) -> p q n", q=2), AX_X,
                                              ALU.max, negate=True).then_inc(max_ready, 1)
                        else:
                            dve.tensor_reduce(neg_max[:, u % 2, 0:1], flat[:, 512 * sb:512 * sb + T], AX_X, ALU.max, negate=True).then_inc(max_ready, 1)
                    elif e[0] == "trP":
                        u, (h, t) = e[1], e[2]
                        if scaled < u:
                            scale_probs(u, t)
                            scaled = u
                        if t >= 0:
                            dve.wait_ge(trB, l * INCS["trB"] + nB + 1)
                            if u >= 2:
                                dve.wait_ge(pv_pe, l * INCS["pv_pe"] + u - 1)
                            dve.tensor_copy(p_T[:, u % 2, 4:6, :], banks[:, 3, 0:256].rearrange("p (k n) -> p k n", k=2))\
                                .then_inc(trB_out, 1)
                            nB += 1
                    elif e[0] == "ssd":
                        cc = e[1]
                        dve.wait_ge(ecum_ready, l * INCS["ecum_ready"] + 2 * n_y + 1)
                        for h in range(HEADS):
                            ins = dve.tensor_scalar(e_in[:, 0, h, :], banks[:, 5, h * P:(h + 1) * P], cs_tok[:, 0, cc, h:h + 1],
                                                    0.0, ALU.subtract, ALU.min)
                        ins.then_inc(d_ready, 1)
                        dve.wait_ge(g_pe, l * INCS["g_pe"] + n_y + 1)
                        for d, tri in ((0, tri_le), (1, tri_ge)):
                            dve.tensor_tensor(g_mask[:, d, :, :], banks[:, 6, 256:512].rearrange("p (g s) -> p g s", g=2),
                                              tri.unsqueeze(1).to_broadcast([P, 2, P]), ALU.mult).then_inc(gm_ready, 1)
                        n_y += 1
                    elif e[0] == "ssd_y":
                        dve.wait_ge(e_ready, l * INCS["e_ready"] + 2 * n_y - 1)
                        dve.wait_ge(gm_ready, l * INCS["gm_ready"] + 2 * n_y)
                        v = e_in[:, 0, :, :].rearrange("p (g r) s -> p g r s", r=2)
                        dve.tensor_tensor(v, v, g_mask[:, 0, :, :].unsqueeze(2).to_broadcast([P, 2, 2, P]), ALU.mult)\
                            .then_inc(w_ready, 1)
                        y_evac(e[1], n_y - 1)
                    elif e[0] == "gz":
                        dve.wait_ge(y_out, l * INCS["y_out"] + 2 * n_y)
                        v = mix[:, 2 + e[1], r0:T]
                        dve.tensor_tensor(v, v, silu_z[:, e[1], r0:T], ALU.mult).then_inc(gz_ready, 1)
                    elif e[0] == "gi":
                        ft, a = e[1], e[2]
                        dve.wait_ge(groot_ready, l * INCS["groot_ready"] + 1)
                        link(dve.reciprocal(gn_r[:, ft, a:a + 256], gn_r[:, ft, a:a + 256]))
                        v = mix[:, 2 + ft, a:a + 256]
                        dve.scalar_tensor_tensor(v, v, vecs[l][:, V_SN + ft:V_SN + ft + 1], gn_r[:, ft, a:a + 256], ALU.mult, ALU.mult)\
                            .then_inc(gn_done, 1)
                for j in range(KC):
                    dve.wait_ge(m_hi_ready, l * INCS["m_hi_ready"] + j + 1)
                    dve.tensor_tensor(h_lo[:, j, r0:T], mix[:, j, r0:T], as_f32(h_hi[:, j, r0:T]), ALU.subtract).then_inc(m_lo_ready, 1)

                for n in range(N_OUT):
                    N = base + N_FEAT + N_TOK + n
                    split_lo(N + 1)
                    gated_add(l, 2, n, N, sp_)
                norm(l, 1, sp_, up_base[l][0])
                for b, nf in enumerate(FF_BLOCKS):
                    nb = up_base[l][b]
                    gb = l * sum(FF_BLOCKS) + sum(FF_BLOCKS[:b])

                    def up(i, first=False):
                        m = pair_use(nb)

                        def g_low(f):
                            dve.wait_ge(g_hi_ready, i * 2 + (gb + f + 1))
                            at = bass.ds(i * (2 * T) + f * T + r0, T - r0)
                            dve.tensor_tensor(g_lo[:, at], g_f[:, f, r0:T], as_f32(g_hi[:, at]), ALU.subtract).then_inc(g_lo_ready, 1)
                        for j in range(4):
                            if not first or j:
                                split_lo(nb + j + 1, i * 4)
                            if j == 2:
                                g_low(0)
                            if j % 2:
                                f = j // 2
                                dve.wait_ge(pair_free[0], i * 2 + (m + f + 1))
                                dve.wait_ge(tile_done, i * 4 + (nb + j + 1))
                                dve.tensor_tensor(g_f[:, f, r0:T], silu_a[:, r0:T], bank_of(1, r0, T), ALU.mult)\
                                    .then_inc(pair_free[1], 1)
                        g_low(1)
                    at = 0
                    if b == 0:
                        up(0, True)
                        at = 1
                        if l < DEPTH - 1:
                            mod_bias(l + 1, 0)
                            up(1)
                            mod_bias(l + 1, 1)
                            make_gain(l + 1, 0)
                            at = 2
                    with dve.Fori(at, nf // 2) as i:
                        up(i)
                    for n in range(KC):
                        N = down_base[l][b] + n
                        if N + 1 < DEPTH * N_TILES:
                            split_lo(N + 1)
                        gated_add(l, 5, n, N, sp_)
            for t in range(SEQ // P):
                dve.wait_ge(o_pe, 2 * t + 2)
                dve.tensor_copy(x_out[:, t, 512:D], banks[:, 2 * (t % 2) + 1, :]).then_inc(out_b, 1)

        @block.tensor
        def _(pe):
            def mod_step(l, part, kc, i=0):
                q = l * N_MOD + part
                s = q * KC + kc
                if kc == 0:
                    if q > 0 or i > 0:
                        pe.wait_ge(rows_ready, i * 4 + 4 * q)
                pe.wait_ge(mod_landed[kc % 4], i * 32 + 16 * (s // 4 + 1))
                for g in range(4):
                    ins = pe.matmul(banks[32 * g:32 * g + 2, 7, 0:256], cond[:, :, kc], mod_ring[kc % 4][:, 256 * g:256 * g + 256],
                                    start=(kc == 0), stop=(kc == KC - 1))
                ins.then_inc(mod_used, 1)

            def mod_turn(l, part, i=0):
                q = l * N_MOD + part
                pe.wait_ge(rows_ready, i * 4 + 4 * (q + 1))
                if q > 0 or i > 0:
                    pe.wait_ge(mods_ready, i * 2 + 2 * q)
                for t in range(2):
                    ins = pe.transpose(banks[:, 6, P * t:P * t + P], mod_rows[:, P * t:P * t + P], ident)
                ins.then_inc(rows_T, 1)

            def sum_over_features(n, sp_):
                pe.wait_ge(acc_ready, n * INCS["acc_ready"] + KC - 2)
                for a, b in sp_:
                    pe.matmul(bank_of(3, a, b), ones, sq_acc[:, a:b], start=True, stop=False)
                pe.wait_ge(sq_ready, n * INCS["sq_ready"] + KC)
                for a, b in sp_:
                    ins = pe.matmul(bank_of(3, a, b), ones, sq[:, (KC - 1) % 2, a:b], start=False, stop=True)
                ins.then_inc(ss_ready, 1)

            def dense(n, x_hi, x_lo, n_k, sp_, i=0, chunk_ready=None):
                dense_tiles((n,), x_hi, x_lo, n_k, (sp_,), i, chunk_ready)

            def dense_tiles(tiles, x_hi, x_lo, n_k, spans_, i=0, chunk_ready=None):
                for n in tiles:
                    pe.wait_ge(lo_ready, i * 4 + (n + 1))
                    if pair_use(n) > 0 or i > 0:
                        pe.wait_ge(pair_free[n % 2], i * 2 + pair_use(n))
                for k in range(n_k):
                    if chunk_ready is not None:
                        pe.wait_ge(chunk_ready[0], chunk_ready[1] + k + 1)
                    w = slice(k * P, (k + 1) * P)
                    for n, sp_ in zip(tiles, spans_):
                        p = n % 2
                        for q, (ws, xs) in enumerate(((w_hi, x_hi), (w_hi, x_lo), (w_lo, x_hi))):
                            for a, b in sp_:
                                ins = pe.matmul(bank_of(p, a, b), ws[p][:, w], xs(k, a, b), start=(k == 0 and q == 0),
                                                stop=(k == n_k - 1 and q == 2))
                        if k == n_k - 1:
                            ins.then_inc(tile_done, 1)

            def h_of(t):
                return lambda k, a, b: t[:, k, a:b]

            def g_of(t):
                return lambda k, a, b: t[:, k * T + a:k * T + b]

            def mod_steps(j, l, part, i=0):
                for s in range(STEPS_AT[j]):
                    mod_step(l, part, sum(STEPS_AT[:j]) + s, i)

            def vectors(l):
                pe.wait_ge(vrows_landed[l], 16 * (9 if l == 0 else 7))
                pe.transpose(banks[:, 4 + l, 0:N_VEC[l]], vrows[l][0:N_VEC[l], :], ident[0:N_VEC[l], 0:N_VEC[l]]).then_inc(vec_T, 1)

            pe.wait_ge(ident_landed, 16)
            vectors(0)
            pe.wait_ge(cond_ready, 1)
            slabs = [(part, kc) for part in range(2) for kc in range(KC)]
            for t in range(TT):
                pe.wait_ge(x_landed[t], 16)
                if t >= 2:
                    pe.wait_ge(xT_a, t - 1)
                    pe.wait_ge(xT_b, t - 1)
                for k in range(KC):
                    ins = pe.transpose(banks[:, 2 * (t % 2) + k // 4, (k % 4) * P:(k % 4 + 1) * P], x_in[:, t, k * P:(k + 1) * P], ident)
                    if k % 4 == 3:
                        ins.then_inc(xT_pe, 1)
                for _ in range(2):
                    part, kc = slabs.pop(0)
                    mod_step(0, part, kc)
                    if kc == KC - 1:
                        mod_turn(0, part)
            for part, kc in slabs:
                mod_step(0, part, kc)
                if kc == KC - 1:
                    mod_turn(0, part)
            pe.wait_ge(table_landed, 16)
            vectors(1)
            pe.wait_ge(xT_a, TT)
            pe.wait_ge(xT_b, TT)

            for l in range(DEPTH):
                base = tile_base[l]
                sp_ = spans(l)
                both = [(0, CTX), (CTX, T)]
                pe.wait_ge(mods_ready, 2 * (l * N_MOD + 2))
                sum_over_features(2 * l, both)
                dense_tiles((base, base + 1), h_of(h_hi), h_of(h_lo), KC, (sp_, sp_), chunk_ready=(h_lo_ready, 2 * l * KC))
                for n in range(N_FEAT):
                    if n >= 2:
                        dense(base + n, h_of(h_hi), h_of(h_lo), KC, both if n < 6 else sp_)
                    mod_steps(n % 4, l, 2 + n // 4)
                    if n % 4 == 3:
                        mod_turn(l, 2 + n // 4)
                for p in range(2):
                    pe.wait_ge(pair_free[p], pair_use(base + N_FEAT))
                def token_blocks(i):
                    for j in range(4):
                        n = base + N_FEAT + j
                        width = 264 if j < 2 else 256
                        half = j % 2
                        pe.wait_ge(lo_ready, i * 4 + (n + 1))
                        for t in range(TT):
                            if half == 0:
                                block_no = 4 * l + j // 2
                                if block_no > 0 or i > 0:
                                    pe.wait_ge(tok_free, i * (2 * TT) + ((block_no - 1) * TT + t + 1))
                            for k in range(4):
                                kk = 4 * half + k
                                for q, (hs, ws) in enumerate(((h_hi, w_hi), (h_lo, w_hi), (h_hi, w_lo))):
                                    ins = pe.matmul(banks[:, t, 0:width], hs[:, kk, t * P:(t + 1) * P],
                                                    ws[n % 2][:, k * width:(k + 1) * width],
                                                    start=(kk == 0 and q == 0), stop=(kk == KC - 1 and q == 2))
                            if half == 1 and t < TT - 1:
                                ins.then_inc(tok_ready, 1)
                        ins.then_inc(tile_done, 1)
                        mod_steps(j, l, 4, i)
                    mod_turn(l, 4, i)
                if l == 0:
                    for i in range(2):
                        token_blocks(i)
                else:
                    with pe.Fori(0, 2) as i:
                        token_blocks(i)

                ev, units, two_buffers = mixer_events(l)
                nA = nB = n_st = n_y = n_pv = n_gs = 0
                q_job, p_job = {}, {}
                pe.wait_ge(tok_free, (l + 1) * 4 * TT)
                pe.wait_ge(xbc_ready, l * INCS["xbc_ready"] + 5)

                def transposes(jobs):
                    nonlocal nA, nB
                    bank = tr_bank(nA)
                    prior = nA if nA >= 5 else nA - 1
                    if prior > 0:
                        pe.wait_ge(trA_out, l * INCS["trA_out"] + prior)
                        if nB:
                            pe.wait_ge(trB_out, l * INCS["trB_out"] + (nB if nA >= 5 else nB - 1))
                    for k, src in enumerate(jobs):
                        ins = pe.transpose(banks[:, bank + k // 4, (k % 4) * P:(k % 4 + 1) * P], src, ident)
                        if k == 3:
                            ins.then_inc(trA, 1)
                        elif k == 5:
                            ins.then_inc(trB, 1)
                    nA += 1
                    nB += len(jobs) > 4

                for e in ev:
                    if e[0] == "tr" and e[1] in ("x", "b"):
                        src = x_T[:, e[2], :] if e[1] == "x" else b_T[:, :]
                        transposes([src[:, t * P:(t + 1) * P] for t in range(TT)])
                    elif e[0] == "tr" and e[1] == "k":
                        pe.wait_ge(qk_ready, l * INCS["qk_ready"] + 3)
                        transposes([qk[:, 2, t, e[2] * P:(e[2] + 1) * P] for t in range(TT)])
                        k_job = nA, nB
                    elif e[0] == "tr":
                        pe.wait_ge(qk_ready, l * INCS["qk_ready"] + e[2] // 2 + 1)
                        q_job[e[2]] = nA + 1, nB + (l < DEPTH - 1)
                        order = [2, 3, 4, 5] + ([0, 1] if l < DEPTH - 1 else [])
                        transposes([qk[:, e[2] // 2, t, (e[2] % 2) * P:(e[2] % 2 + 1) * P] for t in order])
                    elif e[0] == "cs":
                        pe.wait_ge(a_ready, l * INCS["a_ready"] + 1)
                        pe.wait_ge(mods_ready, 2 * (l + 1) * N_MOD)
                        for col, tri, d in ((0, tri_le, 0), (24, tri_ge, 1), (48, tri_gt, 0), (72, tri_lt, 1)):
                            pe.matmul(banks[:, 7, col:col + 24], tri, a_tok[:, :, 4 * d:4 * d + 4], start=True, stop=True)
                        pe.matmul(banks[:, 7, 96:144], ones, a_tok[:, :, :], start=True, stop=True).then_inc(cs_pe, 1)
                    elif e[0] == "pool":
                        pe.wait_ge(cs_ready, l * INCS["cs_ready"] + 3)
                        pe.wait_ge(pooled_ready, l * INCS["pooled_ready"] + e[1] + 1)
                        pe.wait_ge(small_landed, 16 * 9 * DEPTH)
                        for a, b in sp_:
                            src = pool_u[:, e[1], PC0:PC0 + CTX] if a == 0 else pool_u[:, e[1], PL0:PL0 + SEQ]
                            ins = pe.matmul(bank_of(2 + e[1], a, b), pool_bd[l][:, e[1], :], src, start=True, stop=True)
                        ins.then_inc(pm_pe, 1)
                    elif e[0] == "state":
                        _, d, cc, nxt = e
                        pe.wait_ge(pm_out, l * INCS["pm_out"] + 2)
                        pe.wait_ge(xw_ready, l * INCS["xw_ready"] + n_st + 1)
                        if n_st >= 2:
                            pe.wait_ge(st_ready, l * INCS["st_ready"] + n_st - 1)
                        pe.matmul(banks[:, 4 + n_st % 2, 0:256], b_tok[:, cc, :], x_w[:, n_st % 2, :], start=True, stop=True)\
                            .then_inc(st_pe, 1)
                        n_st += 1
                    elif e[0] == "S":
                        u, (h, t) = e[1], e[2]
                        pe.wait_ge(trA_out, l * INCS["trA_out"] + max(q_job[h][0], k_job[0]))
                        pe.wait_ge(trB_out, l * INCS["trB_out"] + max(q_job[h][1], k_job[1]))
                        sb = score_bank(u, two_buffers)
                        if u == two_buffers:
                            pe.wait_ge(d_ready, l * INCS["d_ready"] + n_y)
                            pe.wait_ge(d_back_ready, l * INCS["d_back_ready"] + n_y)
                        elif u:
                            pe.wait_ge(exp_ready, l * INCS["exp_ready"] + (u if u < two_buffers else u - 1))
                        k_h = k_T[:, h // 2, :]
                        if t < 0:
                            for q in range(2):
                                ins = pe.matmul(banks[:, sb, 256 * q:256 * q + 256], q_T[:, h % 2, q * P:(q + 1) * P], k_h[:, 0:CTX],
                                                start=True, stop=True)
                        else:
                            q_t = q_T[:, h % 2, CTX + t * P:CTX + (t + 1) * P]
                            pe.matmul(banks[:, sb, :], q_t, k_h[:, 0:512], start=True, stop=True)
                            ins = pe.matmul(banks[:, sb + 1, 0:256], q_t, k_h[:, 512:T], start=True, stop=True)
                        ins.then_inc(s_ready, 1)
                    elif e[0] == "trP":
                        u, (h, t) = e[1], e[2]
                        pe.wait_ge(p_ready, l * INCS["p_ready"] + u + 1)
                        pv = probs[:, u % 3, :]
                        transposes([pv[:, k * P:(k + 1) * P] for k in range(4 if t < 0 else 6)])
                        p_job[u] = nA, nB
                    elif e[0] == "PV":
                        u, (h, t) = e[1], e[2]
                        pe.wait_ge(trA_out, l * INCS["trA_out"] + p_job[u][0])
                        pe.wait_ge(trB_out, l * INCS["trB_out"] + p_job[u][1])
                        if n_pv and t <= 0:
                            pe.wait_ge(pv_out, l * INCS["pv_out"] + n_pv)
                        g = h // 2
                        for k in range(2 if t < 0 else TT):
                            if t < 0:
                                dst, rhs = banks[:, 7, 0:CTX], p_T[:, u % 2, 2 * k:2 * k + 2, :].rearrange("p q n -> p (q n)")
                            else:
                                dst, rhs = banks[:, 7, t * P:(t + 1) * P], p_T[:, u % 2, k, :]
                            ins = pe.matmul(dst, v_tok[:, k, g * P:(g + 1) * P], rhs, start=(k == 0), stop=(k == (1 if t < 0 else TT - 1)))
                        ins.then_inc(pv_pe, 1)
                        n_pv += t < 0 or t == SEQ // P - 1
                    elif e[0] == "ssd":
                        cc = e[1]
                        if n_y == 0:
                            pe.wait_ge(pads_zero, l * INCS["pads_zero"] + 8)
                            pe.wait_ge(st_ready, l * INCS["st_ready"] + n_st)
                        for d in range(DIRS):
                            if n_y:
                                pe.wait_ge((d_ready, d_back_ready)[d], l * INCS["d_ready"] + n_y)
                            for h in range(HEADS):
                                ins = pe.matmul(banks[:, 5 - d, h * P:(h + 1) * P], a_tok[:, cc, 4 * d + h:4 * d + h + 1].to_broadcast([P, P]),
                                                (tri_le, tri_ge)[d], start=True, stop=True)
                            ins.then_inc(cb_pe, 1)
                        if n_y:
                            pe.wait_ge(y_out, l * INCS["y_out"] + 2 * n_y)
                        pe.matmul(banks[:, 6, 256:512].rearrange("p (g s) -> p g s", g=2), b_T[:, cc * P:(cc + 1) * P],
                                  c_T[:, :, cc * P:(cc + 1) * P], start=True, stop=True).then_inc(g_pe, 1)
                        n_y += 1
                    elif e[0] == "ssd_y":
                        cc = e[1]
                        pe.wait_ge(w_ready, l * INCS["w_ready"] + n_y)
                        pe.wait_ge(w_back_ready, l * INCS["w_back_ready"] + n_y)
                        pe.wait_ge(cdec_ready, l * INCS["cdec_ready"] + 2 * n_y)
                        for h in range(HEADS):
                            dst = banks[64 * (h % 2):64 * (h % 2) + 64, 6, (h // 2) * P:(h // 2 + 1) * P]
                            terms = [(x_dt[:, d, 64 * h:64 * h + 64], e_in[:, d, h, :]) for d in range(DIRS)]
                            terms += [(h_prev[:, d, cc, 64 * h:64 * h + 64], e_cum[:, d, h, :]) for d in range(DIRS) if cc != (0, 1)[d]]
                            for k, (lhs, rhs) in enumerate(terms):
                                ins = pe.matmul(dst, lhs, rhs, start=(k == 0), stop=(k == len(terms) - 1))
                        ins.then_inc(y_pe, 1)
                    elif e[0] == "gs":
                        a, b = sp_[e[2]]
                        pe.wait_ge(gsq_ready, l * INCS["gsq_ready"] + e[1] + 1)
                        if n_gs:
                            pe.wait_ge(gss_out, l * INCS["gss_out"] + n_gs)
                        else:
                            pe.wait_ge(y_out, l * INCS["y_out"] + 2 * n_y)
                        pe.matmul(banks[:, 6, 0:b - a], ones, gn_sq[:, a:b], start=True, stop=True).then_inc(gss_pe, 1)
                        n_gs += 1

                for n in range(0, N_OUT, 4):
                    for j in range(4):
                        dense(base + N_FEAT + N_TOK + n + j, h_of(h_hi), h_of(h_lo), KC, sp_,
                              chunk_ready=(m_lo_ready, l * KC) if n + j == 0 else None)
                sum_over_features(2 * l + 1, sp_)
                for b, nf in enumerate(FF_BLOCKS):
                    nb = up_base[l][b]

                    def up(i, with_mod=False, first=False):
                        if first:
                            dense_tiles((nb, nb + 1), h_of(h_hi), h_of(h_lo), KC, (sp_, sp_), i, (h_lo_ready, (2 * l + 1) * KC))
                        for j in range(4):
                            if not first or j >= 2:
                                dense(nb + j, h_of(h_hi), h_of(h_lo), KC, sp_, i)
                            if with_mod:
                                mod_steps(j, l + 1, 0, i)
                        if with_mod:
                            mod_turn(l + 1, 0, i)
                    at = 0
                    if b == 0:
                        up(0, l < DEPTH - 1, True)
                        at = 1
                        if l < DEPTH - 1:
                            up(1, True)
                            at = 2
                    with pe.Fori(at, nf // 2) as i:
                        up(i)
                    hidden = (g_lo_ready, l * sum(FF_BLOCKS) + sum(FF_BLOCKS[:b]))
                    with pe.Fori(0, 2) as i:
                        for j in range(4):
                            dense(down_base[l][b] + j, g_of(g_hi), g_of(g_lo), nf, sp_, i, hidden if j == 0 else None)
            for p in range(2):
                pe.wait_ge(pair_free[p], DEPTH * (N_TILES - N_TOK) // 2)
            for t in range(SEQ // P):
                if t >= 2:
                    pe.wait_ge(out_a, t - 1)
                    pe.wait_ge(out_b, t - 1)
                for k in range(KC):
                    ins = pe.transpose(banks[:, 2 * (t % 2) + k // 4, (k % 4) * P:(k % 4 + 1) * P],
                                       x_res[:, k, CTX + t * P:CTX + (t + 1) * P], ident)
                    if k % 4 == 3:
                        ins.then_inc(o_pe, 1)


_INS = ['x', 'c', 'ctx', 'c_ctx', 'norm1_w', 'norm2_w', 'w_mod', 'b_mod', 'w_in', 'pool_w', 'pool_scale', 'conv_w', 'conv_b',
        'dt_bias', 'a_log', 'd_skip', 'ssd_norm_w', 'q_norm_w', 'k_norm_w', 'w_out', 'w1', 'w3', 'w2']
_OUTS = [((1, SEQ, D), 'float32')]


def kernel(**inputs):
    import numpy as _np
    import concourse.bacc as _bacc
    from concourse import mybir as _mybir
    from concourse.bass_utils import run_bass_kernel_spmd as _run

    nc = _bacc.Bacc("TRN2", target_bir_lowering=False, num_devices=1, dynamic_dma_scratch_size=1024)
    table, count = shape_constants()
    arrays, args = {}, []
    for name, a in [(n, inputs[n]) for n in _INS] + [("table", table), ("count", count)]:
        a = _np.ascontiguousarray(a)
        arrays[f"in_{name}_dram"] = a
        args.append(nc.dram_tensor(f"in_{name}_dram", a.shape, _mybir.dt.from_np(a.dtype), kind="ExternalInput").ap())
    for i, (shape, dtype) in enumerate(_OUTS):
        dt = _mybir.dt.from_np(_np.dtype(dtype))
        args.append(nc.dram_tensor(f"out_{i}_dram", shape, dt, kind="ExternalOutput").ap())
    hybrid_kernel(nc, *args)
    r = _run(nc, [arrays], core_ids=[0])
    got = tuple(r.results[0][f"out_{i}_dram"] for i in range(len(_OUTS)))
    return got[0]
```

```python
from contextlib import ExitStack

import numpy as np

import concourse.bass as bass
from concourse import mybir

ALU = mybir.AluOpType
ACT = mybir.ActivationFunctionType
F32 = mybir.dt.float32
F32R = mybir.dt.float32r
AX_X = mybir.AxisListType.X

P = 128
D = 1024
KC = D // P
CTX, SEQ = 256, 512
T = CTX + SEQ
TT = T // P
DEPTH = 2
EPS = 1e-6
GRID_W = 64
N_MOD = 6
POOL_DIM = 256
SSD_INNER = 256
HEADS = 4
HD_SSD = 64
DIRS = 2
ATT_HEADS, KV_HEADS, HEAD_DIM = 4, 2, 128
D_FF = 2816
OFF_POOL, OFF_Z, OFF_XBC, OFF_TOK = 0, 256, 512, 1024
N_DT = DIRS * HEADS
D_IN = OFF_TOK + N_DT + ATT_HEADS * HEAD_DIM + 2 * KV_HEADS * HEAD_DIM
PAD = 8
PW = PAD + CTX + 2 * PAD + SEQ + PAD
PC0, PL0 = PAD, PAD + CTX + 2 * PAD
POOL_WINDOWS = (2, 4, 8, 16)

N_FEAT = 8
N_TOK = 8
N_OUT = 8
FF_BLOCKS = (8, 8, 6)
N_TILES = N_FEAT + N_TOK + N_OUT + sum(2 * f + KC for f in FF_BLOCKS)
WT = 4 * 264
FEAT_COLS = (0, 128, 512, 640, 768, 896, 256, 384)
V_BMOD, V_N1, V_N2, V_PS, V_CB, V_CW, V_SN, V_C = 0, 48, 56, 64, 66, 70, 90, 92
N_VEC = (V_C + 2 * KC, V_C)

UNITS = ATT_HEADS * (SEQ // P + 1)
TR_A = 2 + 1 + KV_HEADS + ATT_HEADS + UNITS
TR_B = TR_A - ATT_HEADS
STATES = DIRS * (TT - 1)
INCS = dict(
    sq_ready=KC, acc_ready=KC - 2, ss_ready=1, root_ready=1, rstd_ready=1, rstd_pe=1, t_ready=KC, h_hi_ready=KC,
    h_lo_ready=KC, xbc_ready=5, pads_zero=8, count_used=2, pooled_ready=2, qksq_ready=3, qkss_ready=3,
    qkrt_ready=3, qkn_ready=3, rope_s_ready=6, qk_ready=3, dt_in=1, dt_exp=2, a_ready=1, cs_pe=1, cs_ready=3,
    ws_ready=1, trA=TR_A, trA_out=TR_A, trB=TR_B, trB_out=TR_B, xw_ready=STATES, st_pe=STATES, st_ready=STATES,
    pm_pe=2, pm_out=2, s_ready=UNITS, max_ready=UNITS, exp_ready=UNITS, p_ready=UNITS, pv_pe=UNITS,
    pv_out=2 * ATT_HEADS, g_pe=TT, cb_pe=2 * TT, gm_ready=2 * TT, d_ready=TT, d_back_ready=TT, ecum_ready=2 * TT,
    e_ready=2 * TT, w_ready=TT, w_back_ready=TT, cdec_ready=2 * TT, xdt_ready=2 * TT, y_pe=TT, y_out=2 * TT, gz_ready=2,
    gsq_ready=2, gss_pe=4, gss_out=4, groot_ready=1, gn_done=6, m_hi_ready=KC, m_lo_ready=KC,
)


def shape_constants():
    j = np.arange(P)
    ident = np.eye(P)
    le = (j[:, None] <= j[None, :]).astype(np.float64)
    ge = (j[:, None] >= j[None, :]).astype(np.float64)
    gt = (j[:, None] > j[None, :]).astype(np.float64)
    lt = (j[:, None] < j[None, :]).astype(np.float64)
    ones = np.ones((P, P))
    axis_dim = HEAD_DIM // 2
    inv = 10000.0 ** (-np.arange(0, axis_dim, 2) / axis_dim)
    t = np.arange(SEQ)
    ang = np.stack([(t // GRID_W)[:, None] * inv, (t % GRID_W)[:, None] * inv], 1)
    cos, sin = np.cos(ang), np.sin(ang)
    rc = np.concatenate([cos, cos], 2).reshape(SEQ, HEAD_DIM)
    rs = np.concatenate([-sin, sin], 2).reshape(SEQ, HEAD_DIM)
    rc = np.tile(rc.reshape(SEQ // P, P, 1, HEAD_DIM).transpose(1, 0, 2, 3), (1, 1, 2, 1)).reshape(P, -1)
    rs = np.tile(rs.reshape(SEQ // P, P, 1, HEAD_DIM).transpose(1, 0, 2, 3), (1, 1, 2, 1)).reshape(P, -1)
    table = np.concatenate([ident, le, ge, gt, lt, ones, rc, rs], 1).astype(np.float32)
    count = np.zeros((2, P, PW), np.float32)
    for f in range(2):
        for half in range(2):
            w = POOL_WINDOWS[2 * f + half]
            for start, n in ((PC0, CTX), (PL0, SEQ)):
                t = np.arange(n)
                lo, hi = np.clip(t - w // 2, 0, n), np.clip(t - w // 2 + w, 0, n)
                count[f, 64 * half:64 * half + 64, start:start + n] = 1.0 / (hi - lo)
    return table, count


class OwnOrder:

    def __init__(self, sem):
        self.sem, self.n, self.i, self.per, self.base = sem, 0, None, 0, 0

    def loop(self, i, per):
        self.i, self.per, self.base = i, per, self.n

    def end(self, count):
        assert self.n - self.base == self.per, (self.n - self.base, self.per)
        self.n, self.i = self.base + self.per * count, None

    def mark(self, ins):
        ins.then_inc(self.sem, 1)
        self.n += 1
        return self.n if self.i is None else self.i * self.per + self.n


def hybrid_kernel(nc, x, c, ctx, c_ctx, norm1_w, norm2_w, w_mod, b_mod, w_in, pool_w, pool_scale, conv_w,
                  conv_b, dt_bias, a_log, d_skip, ssd_norm_w, q_norm_w, k_norm_w, w_out, w1, w3, w2,
                  table, count, out):
    with ExitStack() as stack:
        usable = nc.sbuf_usable_end - nc.sbuf_base - 64
        stack.enter_context(nc.sbuf_tensor("arena", [P, usable // 4], F32))
        start = -(-(nc.sbuf_usable_end - usable) // 64) * 64
        start = (nc.sbuf_base - (usable // 4) * 4) // 64 * 64 + 64
        place = [start]

        def put(name, shape, dt=F32, at=None):
            size = 4 * int(np.prod(shape[1:]))
            if at is None:
                at, place[0] = place[0], place[0] + (size + 31) // 32 * 32
            assert at + size <= nc.sbuf_usable_end, (name, at, size)
            return nc.alloc_sbuf_tensor_at(name, shape, dt, offset=at)

        x_res = put("x_res", [P, KC, T])
        H0 = place[0]
        h_hi = put("h_hi", [P, KC, T], F32R)
        h_lo = put("h_lo", [P, KC, T], F32R)
        raw = [put(f"raw{s}", [P, WT]) for s in range(4)]
        w_hi = [put(f"w_hi{s}", [P, WT], F32R) for s in range(2)]
        w_lo = [put(f"w_lo{s}", [P, WT], F32R) for s in range(2)]
        M0 = place[0]
        mod_ring = [put(f"mod_ring{s}", [P, D]) for s in range(4)]
        tab = put("tab", [P, 6 * P + 2048])
        ident, tri_le, tri_ge, tri_gt, tri_lt, ones = (tab[:, i * P:(i + 1) * P] for i in range(6))
        rope_c, rope_s = tab[:, 768:1792], tab[:, 1792:2816]
        vecs = [put(f"vecs{l}", [P, 112]) for l in range(DEPTH)]
        cond = put("cond", [P, 2, KC])
        mod_rows = put("mod_rows", [P, 256])
        mods = [put(f"mods{l}", [P, N_MOD, 2, KC]) for l in range(DEPTH)]
        gain = [put(f"gain{l}", [P, 2, 2, KC]) for l in range(DEPTH)]
        dt_b = [put(f"dt_b{l}", [P, N_DT]) for l in range(DEPTH)]
        neg_a = [put(f"neg_a{l}", [P, N_DT]) for l in range(DEPTH)]
        qk_w = [put(f"qk_w{l}", [P, 2, HEAD_DIM]) for l in range(DEPTH)]
        skip2 = [put(f"skip2{l}", [P, 2 * HEADS]) for l in range(DEPTH)]
        skip = [put(f"skip{l}", [P, 2]) for l in range(DEPTH)]
        pool_bd = [put(f"pool_bd{l}", [P, 2, P]) for l in range(DEPTH)]
        eps = put("eps", [P, 1])
        dt_raw = put("dt_raw", [P, TT, N_DT])
        dt_m = put("dt_m", [P, TT, N_DT])
        dt_n = put("dt_n", [P, TT, N_DT])
        dts = put("dts", [P, TT, N_DT])
        a_tok = put("a_tok", [P, TT, N_DT])
        cs_tok = put("cs_tok", [P, DIRS, TT, HEADS])
        decay = put("decay", [P, DIRS, TT, HEADS])
        decay_all = put("decay_all", [P, TT, N_DT])
        w_state = put("w_state", [P, DIRS, TT, HEADS])
        qk_ss = put("qk_ss", [P, 3, 12])
        qk_rt = put("qk_rt", [P, 3, 12])
        neg_max = put("neg_max", [P, 2, 2])
        p_sum = put("p_sum", [P, 2, 2])
        p_inv = put("p_inv", [P, 2, 2])
        G0 = place[0]
        qk = put("qk", [P, 3, TT, 256])
        v_tok = put("v_tok", [P, TT, 256])
        silu_z = put("silu_z", [P, 2, T])
        b_T = put("b_T", [P, T])
        c_T = put("c_T", [P, 2, T])
        X0 = place[0]
        x_tok = put("x_tok", [P, TT, 256])
        b_tok = put("b_tok", [P, TT, P])
        MX0 = place[0]
        mix = put("mix", [P, 8, T])
        END = place[0]
        conv_acc = put("conv_acc", [P, 2, T], at=X0)
        
        pool_u = put("pool_u", [P, 2, PW], at=MX0)
        win_a = put("win_a", [P, PW], at=MX0 + 8 * PW)
        win_b = put("win_b", [P, PW], at=MX0 + 12 * PW)
        inv_n = put("inv_n", [P, PW], at=MX0 + 16 * PW)
        rope_t = put("rope_t", [P, 1024], at=MX0 + 8 * PW)
        qk_sq = put("qk_sq", [P, 12, P], at=MX0 + 8 * PW + 4096)
        x_T = put("x_T", [P, 2, T], at=MX0 + 6 * 4 * T)
        assert 8 * PW + 4096 + 6144 <= 6 * 4 * T
        assert 20 * PW <= 6 * 4 * T
        w3_hi = [put("w3_hi0", [P, WT], F32R, at=G0), put("w3_hi1", [P, WT], F32R, at=G0 + 48 * T)]
        w3_lo = [put("w3_lo0", [P, WT], F32R, at=G0 + 4 * WT), put("w3_lo1", [P, WT], F32R, at=G0 + 48 * T + 4 * WT)]
        g_hi = put("g_hi", [P, 8 * T], F32R, at=G0)
        g_lo = put("g_lo", [P, 8 * T], F32R, at=G0 + 32 * T)
        silu_a = put("silu_a", [P, T], at=G0 + 64 * T)
        g_f = put("g_f", [P, 2, T], at=G0 + 68 * T)
        N0 = END - 24 * T
        assert N0 >= G0 + 48 * T and N0 >= X0
        sq = put("sq", [P, 2, T], at=N0)
        sq_acc = put("sq_acc", [P, T], at=N0 + 8 * T)
        rstd = put("rstd", [P, T // 4], at=N0 + 12 * T)
        nrm = put("nrm", [P, 2, T], at=N0 + 16 * T)
        assert G0 + 76 * T <= END
        x_in = put("x_in", [P, TT, D], at=G0)
        vrows = [put(f"vrows{l}", [P, P], at=G0 + 4 * TT * D + 512 * l) for l in range(DEPTH)]
        x_out = put("x_out", [P, KC, SEQ // P, P], at=H0)
        p_T = put("p_T", [P, 2, TT, P], at=H0)
        k_T = put("k_T", [P, KV_HEADS, T], at=H0 + 12288)
        q_T = put("q_T", [P, 2, T], at=H0 + 18432)
        S0 = H0 + 24576
        probs = put("probs", [P, 3, T], at=S0)
        e_in = put("e_in", [P, DIRS, HEADS, P], at=S0 + 9216)
        e_cum = put("e_cum", [P, DIRS, HEADS, P], at=S0 + 13312)
        g_mask = put("g_mask", [P, DIRS, 2, P], at=S0 + 17408)
        x_dt = put("x_dt", [P, DIRS, 256], at=S0 + 19456)
        x_w = put("x_w", [P, 2, 256], at=S0 + 21504)
        gn_sq = put("gn_sq", [P, T], at=S0 + 9216)
        gn_r = put("gn_r", [P, 2, T], at=S0 + 12288)
        h_prev = put("h_prev", [P, DIRS, TT, 256], at=M0)

        banks = stack.enter_context(nc.psum_tensor("banks", [P, 8, 512], F32))
        flat = banks[:, :, :].rearrange("p b n -> p (b n)")

        def sem(name):
            return stack.enter_context(nc.semaphore(name))

        raw_landed = [sem(f"raw_landed{s}") for s in range(4)]
        mod_landed = [sem(f"mod_landed{s}") for s in range(4)]
        vrows_landed = [sem(f"vrows_landed{l}") for l in range(DEPTH)]
        ident_landed, table_landed = sem("ident_landed"), sem("table_landed")
        x_landed = [sem(f"x_landed{t}") for t in range(TT)]
        small_landed = sem("small_landed")
        dt_landed = [sem(f"dt_landed{half}") for half in range(2)]
        count_landed = sem("count_landed")
        out_stored = sem("out_stored")
        hi_ready, lo_ready, tile_done = sem("hi_ready"), sem("lo_ready"), sem("tile_done")
        pair_free = [sem("pair_free0"), sem("pair_free1")]
        tok_ready, tok_free = sem("tok_ready"), sem("tok_free")
        g_hi_ready, g_lo_ready = sem("g_hi_ready"), sem("g_lo_ready")
        mod_used, rows_ready, rows_T, mods_ready, gain_ready = (
            sem(n) for n in ("mod_used", "rows_ready", "rows_T", "mods_ready", "gain_ready"))
        zeroed, vec_T, vec_ready, cond_ready = (sem(n) for n in ("zeroed", "vec_T", "vec_ready", "cond_ready"))
        xT_pe, xT_a, xT_b, small_act, small_ready = (
            sem(n) for n in ("xT_pe", "xT_a", "xT_b", "small_act", "small_ready"))
        s_dve, s_act, s_pool = sem("dve_order"), sem("act_order"), sem("pool_order")
        sq_ready = sem("sq_ready")
        acc_ready = sem("acc_ready")
        ss_ready = sem("ss_ready")
        root_ready = sem("root_ready")
        rstd_ready, rstd_pe = sem("rstd_ready"), sem("rstd_pe")
        t_ready = sem("t_ready")
        h_hi_ready = sem("h_hi_ready")
        h_lo_ready = sem("h_lo_ready")
        xbc_ready = sem("xbc_ready")
        pads_zero = sem("pads_zero")
        count_used = sem("count_used")
        pooled_ready = sem("pooled_ready")
        qksq_ready = sem("qksq_ready")
        qkss_ready = sem("qkss_ready")
        qkrt_ready = sem("qkrt_ready")
        qkn_ready = sem("qkn_ready")
        rope_s_ready = sem("rope_s_ready")
        qk_ready = sem("qk_ready")
        dt_in = sem("dt_in")
        dt_exp = sem("dt_exp")
        a_ready = sem("a_ready")
        cs_pe = sem("cs_pe")
        cs_ready = sem("cs_ready")
        ws_ready = sem("ws_ready")
        trA, trB = sem("trA"), sem("trB")
        trA_out, trB_out = sem("trA_out"), sem("trB_out")
        xw_ready = sem("xw_ready")
        st_pe = sem("st_pe")
        st_ready = sem("st_ready")
        pm_pe, pm_out = sem("pm_pe"), sem("pm_out")
        s_ready = sem("s_ready")
        max_ready = sem("max_ready")
        exp_ready = sem("exp_ready")
        p_ready = sem("p_ready")
        pv_pe, pv_out = sem("pv_pe"), sem("pv_out")
        g_pe, cb_pe = sem("g_pe"), sem("cb_pe")
        gm_ready = sem("gm_ready")
        d_ready, d_back_ready = sem("d_ready"), sem("d_back_ready")
        ecum_ready = sem("ecum_ready")
        e_ready = sem("e_ready")
        w_ready, w_back_ready = sem("w_ready"), sem("w_back_ready")
        cdec_ready = sem("cdec_ready")
        xdt_ready = sem("xdt_ready")
        y_pe, y_out = sem("y_pe"), sem("y_out")
        gz_ready = sem("gz_ready")
        gsq_ready = sem("gsq_ready")
        gss_pe, gss_out = sem("gss_pe"), sem("gss_out")
        groot_ready = sem("groot_ready")
        gn_done = sem("gn_done")
        m_hi_ready, m_lo_ready = sem("m_hi_ready"), sem("m_lo_ready")
        o_pe = sem("o_pe")
        out_ready = sem("out_ready")

        def lat0(l):
            return CTX if l == DEPTH - 1 else 0

        def spans(l):
            return [(CTX, T)] if l == DEPTH - 1 else [(0, CTX), (CTX, T)]

        def bank_of(p, a, b):
            return flat[:, 1024 * p + 256 + a:1024 * p + 256 + b]

        def rstd_view(r0):
            return banks[:, 4:6, 0:(T - r0) // 2]

        def tr_bank(k):
            return 2 if k % 2 == 0 or k >= 5 else 0

        tile_base = [l * N_TILES for l in range(DEPTH)]
        up_base, down_base = [], []
        for l in range(DEPTH):
            n = tile_base[l] + N_FEAT + N_TOK + N_OUT
            ub, db = [], []
            for f in FF_BLOCKS:
                ub.append(n)
                db.append(n + 2 * f)
                n += 2 * f + KC
            up_base.append(ub)
            down_base.append(db)

        TOK_COLS = (OFF_TOK + N_DT + 512, OFF_TOK + N_DT + 768, OFF_TOK + N_DT, OFF_TOK + N_DT + 256)

        def tok_from(l, st):
            return CTX // P if l == DEPTH - 1 and st >= 2 else 0

        def tok_count(l, st, signals=False):
            before = [(k, q) for k in range(l + 1) for q in range(4) if (k, q) < (l, st)]
            return sum(TT - tok_from(k, q) - signals for k, q in before)

        def pair_use(n):
            l, k = n // N_TILES, n % N_TILES
            return (l * (N_TILES - N_TOK) + (k if k < N_FEAT else k - N_TOK)) // 2 if not (
                N_FEAT <= k < N_FEAT + N_TOK) else (l * (N_TILES - N_TOK) + N_FEAT) // 2

        STEPS_AT = (3, 3, 2, 0)

        def part_base(l, part):
            return (l * N_MOD + part) * KC

        def mixer_events(l):
            fwd, bwd = list(range(TT)), [1, 0, 5, 4, 3, 2]
            chunks = list(range(TT)) if l < DEPTH - 1 else list(range(2, TT))
            states = []
            for k in range(TT - 1):
                states += [("state", 0, fwd[k], fwd[k + 1]), ("state", 1, bwd[k], bwd[k + 1])]
            ev = [("tr", "x", 0), ("tr", "x", 1), ("tr", "b", 0), ("tr", "k", 0), ("tr", "k", 1), ("cs",), ("q23", 0),
                  ("pool", 0), ("pool", 1), ("q23", 1), ("tr", "q", 0)]
            ev += states[:2] + [("q23", 2)] + states[2:4] + [("q23", 3)]
            states = states[4:]
            units = []
            for h in range(ATT_HEADS):
                if l < DEPTH - 1:
                    units.append((h, -1))
                units += [(h, t) for t in range(SEQ // P)]
            n_sp = len(spans(l))
            gates = []
            for ft in range(2):
                gates += [("gz", ft)] + [("gs", ft, k) for k in range(n_sp)]
            gates += [("gr",)] + [("gi", ft, a) for ft in range(2) for a in range(lat0(l), T, 256)]
            todo = list(chunks)
            last_c, two_buffers = None, None
            for u in range(len(units) + 3):
                if u < len(units):
                    if two_buffers is None and not states and not todo:
                        two_buffers = u
                    ev.append(("S", u, units[u]))
                if 2 <= u < len(units) + 2:
                    ev.append(("trP", u - 2, units[u - 2]))
                if u < len(units):
                    ev.append(("exp", u, units[u]))
                if u >= 3:
                    ev.append(("PV", u - 3, units[u - 3]))
                gate_now = not todo and last_c is None
                if last_c is not None:
                    ev.append(("ssd_y", last_c))
                    last_c = None
                if gate_now and gates and gates[0][0] != "gi":
                    ev.append(gates.pop(0))
                if todo and not states:
                    last_c = todo.pop(0)
                    ev.append(("ssd", last_c))
                for _ in range(4):
                    if states:
                        ev.append(states.pop(0))
                if gate_now and gates:
                    ev.append(gates.pop(0))
                if u < len(units) and units[u][1] == 1 and units[u][0] + 1 < ATT_HEADS:
                    ev.append(("tr", "q", units[u][0] + 1))
            ev += gates
            assert not todo and last_c is None and not states
            return ev, units, two_buffers

        def score_bank(u, two_buffers):
            return 4 if u >= two_buffers and (u - two_buffers) % 2 == 0 else 0

        block = stack.enter_context(nc.Block())

        @block.sync
        def _(sp):
            def vector_rows(l):
                for dst, n, src in (
                    (V_BMOD, 48, b_mod[l].rearrange("(r p) -> r p", p=P)), (V_N1, 8, norm1_w[l].rearrange("(r p) -> r p", p=P)),
                    (V_N2, 8, norm2_w[l].rearrange("(r p) -> r p", p=P)), (V_PS, 2, pool_scale[l].rearrange("(r p) -> r p", p=P)),
                    (V_CB, 4, conv_b[l].rearrange("(r p) -> r p", p=P)), (V_CW, 20, conv_w[l].rearrange("k (r p) -> (k r) p", p=P)),
                    (V_SN, 2, ssd_norm_w[l].rearrange("(r p) -> r p", p=P)),
                ):
                    sp.dma_start(vrows[l][dst:dst + n, :], src).then_inc(vrows_landed[l], 16)
                if l == 0:
                    sp.dma_start(vrows[0][V_C:V_C + 8, :], c[0].rearrange("(r p) -> r p", p=P)).then_inc(vrows_landed[0], 16)
                    sp.dma_start(vrows[0][V_C + 8:V_C + 16, :], c_ctx.rearrange("(r p) -> r p", p=P)).then_inc(vrows_landed[0], 16)

            def load_mod(l, part, kc, slot, used):
                if used is not None:
                    sp.wait_ge(mod_used, used)
                sp.dma_start(mod_ring[slot][:, :], w_mod[l, kc * P:(kc + 1) * P, bass.ds(part * D, D)]).then_inc(mod_landed[slot], 16)

            def load_tile(slot, need_lo, src, n_k, width):
                if need_lo is not None:
                    sp.wait_ge(lo_ready, need_lo)
                dst = raw[slot][:, 0:n_k * width].rearrange("p (k n) -> p k n", k=n_k)
                sp.dma_start(dst, src).then_inc(raw_landed[slot], 16)

            def cols(w, l, col, width=P, k0=0, n_k=KC):
                return w[l].rearrange("(k p) n -> p k n", p=P)[:, k0:k0 + n_k, bass.ds(col, width)]

            def small_parameters():
                def bcast(dst, src):
                    sp.dma_start(dst, src.partition_broadcast(P)).then_inc(small_landed, 16)

                sp.wait_ge(zeroed, 6 + DEPTH)
                for l in range(DEPTH):
                    bcast(dt_b[l][:, :], dt_bias[l].rearrange("d h -> (d h)"))
                    bcast(neg_a[l][:, :], a_log[l].rearrange("d h -> (d h)"))
                    bcast(qk_w[l][:, 0, :], q_norm_w[l])
                    bcast(qk_w[l][:, 1, :], k_norm_w[l])
                    bcast(skip2[l][:, :], d_skip[l].rearrange("d h -> (d h)"))
                    for half in range(2):
                        for ft in range(2):
                            sp.dma_start(pool_bd[l][64 * half:64 * half + 64, ft, 64 * half:64 * half + 64],
                                         pool_w[l, 2 * ft + half]).then_inc(small_landed, 16)

            sp.dma_start(ident, table[:, 0:P]).then_inc(ident_landed, 16)
            vector_rows(0)
            for s in range(2 * KC):
                if s == 4:
                    sp.dma_start(tab[:, P:], table[:, P:]).then_inc(table_landed, 16)
                load_mod(0, s // KC, s % KC, s % 4, s - 3 if s >= 4 else None)
            for l in range(DEPTH):
                base = tile_base[l]
                for n in range(N_FEAT):
                    load_tile(n % 4, base + n - 3 if base + n >= 4 else None, cols(w_in, l, FEAT_COLS[n]), KC, P)
                    if l == 0 and n == 1:
                        vector_rows(1)
                        small_parameters()
                    if n == 2:
                        for k in range(4):
                            load_mod(l, 2, k, k % 4, part_base(l, 2) + k - 3)
                    elif n == 3:
                        for k in range(4, KC):
                            load_mod(l, 2, k, k % 4, part_base(l, 2) + k - 3)
                    elif n >= 4:
                        for s in range(STEPS_AT[n % 4]):
                            k = sum(STEPS_AT[:n % 4]) + s
                            load_mod(l, 3, k, k % 4, part_base(l, 3) + k - 3)
                for n in range(N_TOK):
                    N, st, half = base + N_FEAT + n, n // 2, n % 2
                    width = 264 if st == 0 else 256
                    sp.wait_ge(lo_ready, N - 3)
                    dst = raw[N % 4][:, 0:4 * width].rearrange("p (k n) -> p k n", k=4)
                    if st == 0:
                        sp.dma_start(dst[:, :, 256:264], cols(w_in, l, OFF_TOK, N_DT, 4 * half, 4)).then_inc(dt_landed[half], 16)
                    sp.dma_start(dst[:, :, 0:256], cols(w_in, l, TOK_COLS[st], 256, 4 * half, 4)).then_inc(raw_landed[N % 4], 16)
                    for k in range(sum(STEPS_AT[:n % 4]), sum(STEPS_AT[:n % 4 + 1])):
                        load_mod(l, 4 + n // 4, k, k % 4, part_base(l, 4 + n // 4) + k - 3)
                with sp.Fori(0, 2) as i:
                    nb = base + N_FEAT + N_TOK
                    for j in range(4):
                        load_tile(j, i * 4 + (nb + j - 3), cols(w_out, l, i * (4 * P) + j * P), KC, P)
                f0 = 0
                for b, nf in enumerate(FF_BLOCKS):
                    nb = up_base[l][b]

                    def up(i, with_mod=False):
                        for j in range(4):
                            load_tile(j, i * 4 + (nb + j - 3), cols((w1, w3)[j % 2], l, i * (2 * P) + (f0 + j // 2) * P), KC, P)
                            for s in range(STEPS_AT[j] if with_mod else 0):
                                k = sum(STEPS_AT[:j]) + s
                                load_mod(l + 1, i, k, k % 4, i * KC + (part_base(l + 1, 0) + k - 3))
                    if b == 0 and l < DEPTH - 1:
                        sp.wait_ge(y_pe, l * INCS["y_pe"] + TT)
                        for j in range(4):
                            load_tile(j, nb + j - 3, cols((w1, w3)[j % 2], l, (j // 2) * P), KC, P)
                            if j == 2:
                                for k in range(4):
                                    load_mod(l + 1, 0, k, k % 4, part_base(l + 1, 0) + k - 3)
                        for k in range(4, KC):
                            load_mod(l + 1, 0, k, k % 4, part_base(l + 1, 0) + k - 3)
                        up(1, True)
                        with sp.Fori(2, nf // 2) as i:
                            up(i)
                    else:
                        with sp.Fori(0, nf // 2) as i:
                            up(i)
                    nb2 = down_base[l][b]
                    with sp.Fori(0, 2) as i:
                        for j in range(4):
                            load_tile(j, i * 4 + (nb2 + j - 3), cols(w2, l, i * (4 * P) + j * P, P, f0, nf), nf, P)
                    f0 += nf
            for j in range(KC):
                sp.wait_ge(out_ready, j + 1)
                sp.dma_start(out[0].rearrange("(t p) n -> p t n", p=P)[:, :, j * P:(j + 1) * P], x_out[:, j, :, :]).then_inc(out_stored, 16)
            sp.wait_ge(out_stored, 16 * KC)

        @block.gpsimd
        def _(pool):
            own = OwnOrder(s_pool)

            def link(ins):
                pool.wait_ge(s_pool, own.mark(ins))

            pool.memset(mod_rows[:, :], 0.0).then_inc(zeroed, 1)
            pool.memset(eps[:, :], EPS).then_inc(zeroed, 1)
            for s in range(4):
                pool.memset(raw[s][:, D:WT], 0.0).then_inc(zeroed, 1)
            for l in range(DEPTH):
                pool.memset(pool_bd[l][:, :, :], 0.0).then_inc(zeroed, 1)

            def sum_squares(n, r0):
                for j in range(1, KC - 1):
                    pool.wait_ge(sq_ready, n * INCS["sq_ready"] + j + 1)
                    if j > 1:
                        pool.wait_ge(acc_ready, n * INCS["acc_ready"] + j - 1)
                    in0 = sq[:, 0, r0:T] if j == 1 else sq_acc[:, r0:T]
                    pool.tensor_tensor(sq_acc[:, r0:T], in0, sq[:, j % 2, r0:T], ALU.add).then_inc(acc_ready, 1)

            for l in range(DEPTH):
                r0 = lat0(l)
                if l:
                    sum_squares(2 * l, 0)
                pool.wait_ge(h_lo_ready, (2 * l) * INCS["h_lo_ready"] + KC)
                for ft in range(2):
                    for a, b in ((0, PC0), (PC0 + CTX, PL0), (PL0 + SEQ, PW)):
                        pool.memset(pool_u[:, ft, a:b], 0.0).then_inc(pads_zero, 1)
                pool.wait_ge(pads_zero, l * INCS["pads_zero"] + 6)
                pool.memset(c_T[64:P, 0, :], 0.0).then_inc(pads_zero, 1)
                pool.wait_ge(pads_zero, l * INCS["pads_zero"] + 7)
                pool.memset(c_T[0:64, 1, :], 0.0).then_inc(pads_zero, 1)
                lo = 0 if l < DEPTH - 1 else PL0 - PAD
                w0, w1_ = (PC0 if l < DEPTH - 1 else PL0), PL0 + SEQ
                pool.wait_ge(pads_zero, l * INCS["pads_zero"] + 8)
                for ft in range(2):
                    pool.wait_ge(pair_free[ft], pair_use(tile_base[l] + ft) + 1)
                    u = pool_u[:, ft, :]
                    link(pool.tensor_tensor(win_a[:, lo + 1:PW], u[:, lo:PW - 1], u[:, lo + 1:PW], ALU.add))
                    if ft == 0:
                        link(pool.tensor_tensor(win_b[64:P, lo + 2:PW - 1], win_a[64:P, lo + 1:PW - 2],
                                                win_a[64:P, lo + 3:PW], ALU.add))
                    else:
                        link(pool.tensor_tensor(win_b[:, lo + 2:PW - 1], win_a[:, lo + 1:PW - 2], win_a[:, lo + 3:PW], ALU.add))
                        link(pool.tensor_tensor(win_a[:, lo + 4:PW - 3], win_b[:, lo + 2:PW - 5], win_b[:, lo + 6:PW - 1], ALU.add))
                        link(pool.tensor_tensor(win_b[64:P, lo + 8:PW - 7], win_a[64:P, lo + 4:PW - 11],
                                                win_a[64:P, lo + 12:PW - 3], ALU.add))
                    pool.wait_ge(count_landed, 16 * (2 * l + ft + 1))
                    link(pool.tensor_tensor(win_a[0:64, w0:w1_], win_a[0:64, w0:w1_], inv_n[0:64, w0:w1_], ALU.mult))
                    pool.tensor_tensor(win_a[64:P, w0:w1_], win_b[64:P, w0:w1_], inv_n[64:P, w0:w1_], ALU.mult).then_inc(count_used, 1)
                    pool.wait_ge(count_used, l * INCS["count_used"] + ft + 1)
                    pool.tensor_tensor(u[:, w0:w1_], win_a[:, w0:w1_], u[:, w0:w1_], ALU.subtract).then_inc(pooled_ready, 1)
                    pool.wait_ge(pooled_ready, l * INCS["pooled_ready"] + ft + 1)
                def rotary_sine(seq):
                    blk = (2, 0, 1)[seq]
                    pool.wait_ge(qkn_ready, l * INCS["qkn_ready"] + seq + 1)
                    if seq:
                        pool.wait_ge(qk_ready, l * INCS["qk_ready"] + seq)
                    xv = qk[:, blk, 2:TT, :].rearrange("p t n -> p (t n)").rearrange("p (g h e) -> p g h e", h=2, e=32)
                    sv = rope_s.rearrange("p (g h e) -> p g h e", h=2, e=32)
                    tv = rope_t[:, :].rearrange("p (g h e) -> p g h e", h=2, e=32)
                    for half in range(2):
                        pool.tensor_tensor(tv[:, :, half, :], xv[:, :, 1 - half, :], sv[:, :, half, :], ALU.mult)\
                            .then_inc(rope_s_ready, 1)

                rotary_sine(0)
                rotary_sine(1)
                ev, units, two_buffers = mixer_events(l)
                n_st = n_y = 0
                for e in ev:
                    if e == ("q23", 2):
                        rotary_sine(2)
                    elif e[0] == "state":
                        _, d, cc, _n = e
                        if n_st == 0:
                            pool.wait_ge(ws_ready, l * INCS["ws_ready"] + 1)
                            pool.wait_ge(trA_out, l * INCS["trA_out"] + 3)
                            pool.wait_ge(trB_out, l * INCS["trB_out"] + 3)
                        if n_st >= 2:
                            pool.wait_ge(st_pe, l * INCS["st_pe"] + n_st - 1)
                        pool.tensor_tensor(x_w[:, n_st % 2, :].rearrange("p (h q) -> p h q", h=HEADS),
                                           x_tok[:, cc, :].rearrange("p (h q) -> p h q", h=HEADS),
                                           w_state[:, d, cc, :].unsqueeze(2).to_broadcast([P, HEADS, HD_SSD]), ALU.mult)\
                            .then_inc(xw_ready, 1)
                        n_st += 1
                    elif e[0] == "ssd":
                        cc = e[1]
                        if n_y:
                            pool.wait_ge(y_pe, l * INCS["y_pe"] + n_y)
                        for d in range(DIRS):
                            pool.tensor_tensor(x_dt[:, d, :].rearrange("p (h q) -> p h q", h=HEADS),
                                               x_tok[:, cc, :].rearrange("p (h q) -> p h q", h=HEADS),
                                               dts[:, cc, 4 * d:4 * d + 4].unsqueeze(2).to_broadcast([P, HEADS, HD_SSD]), ALU.mult)\
                                .then_inc(xdt_ready, 1)
                        for d in range(DIRS):
                            pool.wait_ge(ecum_ready, l * INCS["ecum_ready"] + 2 * n_y + d + 1)
                            pool.tensor_tensor(e_cum[:, d, :, :].rearrange("p (g r) s -> p g r s", r=2),
                                               e_cum[:, d, :, :].rearrange("p (g r) s -> p g r s", r=2),
                                               c_T[:, :, cc * P:(cc + 1) * P].unsqueeze(2).to_broadcast([P, 2, 2, P]), ALU.mult)\
                                .then_inc(cdec_ready, 1)
                        pool.wait_ge(e_ready, l * INCS["e_ready"] + 2 * n_y + 2)
                        pool.wait_ge(gm_ready, l * INCS["gm_ready"] + 2 * n_y + 2)
                        v = e_in[:, 1, :, :].rearrange("p (g r) s -> p g r s", r=2)
                        pool.tensor_tensor(v, v, g_mask[:, 1, :, :].unsqueeze(2).to_broadcast([P, 2, 2, P]), ALU.mult)\
                            .then_inc(w_back_ready, 1)
                        n_y += 1
                sum_squares(2 * l + 1, r0)

        @block.scalar
        def _(act):
            own = OwnOrder(s_act)

            def link(ins):
                act.wait_ge(s_act, own.mark(ins))

            act.wait_ge(vrows_landed[0], 16 * 9)
            def load_tokens(t):
                src = ctx[0, t * P:(t + 1) * P, :] if t < CTX // P else x[0, (t - CTX // P) * P:(t - CTX // P + 1) * P, :]
                act.dma_start(x_in[:, t, :], src).then_inc(x_landed[t], 16)

            for t in range(2):
                load_tokens(t)

            def vectors(l):
                act.wait_ge(vec_T, l + 1)
                n = N_VEC[l]
                act.activation(vecs[l][:, 0:n], banks[:, 4 + l, 0:n], ACT.Copy).then_inc(vec_ready, 1)

            def split_hi(n, i4=0):
                act.wait_ge(raw_landed[n % 4], i4 * 4 + 16 * (n // 4 + 1))
                l, k = n // N_TILES, n % N_TILES - N_FEAT
                if k in (0, 1):
                    act.wait_ge(dt_landed[k], 16 * (l + 1))
                if n >= 2:
                    act.wait_ge(tile_done, i4 + (n - 1))
                act.activation(w_hi[n % 2][:, :], raw[n % 4][:, :], ACT.Copy).then_inc(hi_ready, 1)

            def split_third_hi(n, which):
                act.wait_ge(raw_landed[n % 4], 16 * (n // 4 + 1))
                act.activation(w3_hi[which][:, :], raw[n % 4][:, :], ACT.Copy).then_inc(hi_ready, 1)

            def mod_rows_out(q):
                act.wait_ge(mod_used, KC * (q + 1))
                if q:
                    act.wait_ge(rows_T, q)
                for g in range(4):
                    act.activation(mod_rows[32 * g:32 * g + 2, :], banks[32 * g:32 * g + 2, 7, 0:256], ACT.Copy).then_inc(rows_ready, 1)

            def square_chunk(n, j, r0):
                if j >= 2:
                    act.wait_ge(acc_ready, n * INCS["acc_ready"] + max(1, j - 2))
                act.activation(sq[:, j % 2, r0:T], x_res[:, j, r0:T], ACT.Square).then_inc(sq_ready, 1)

            def mean_root(n, r0):
                act.wait_ge(ss_ready, n * INCS["ss_ready"] + 1)
                act.activation(rstd[:, 0:(T - r0) // 4], banks[:, 5, 0:(T - r0) // 4], ACT.Sqrt, bias=eps[:, 0:1], scale=1.0 / D).then_inc(root_ready, 1)

            def norm(l, which, sp_, next_tile):
                n = 2 * l + which
                r0 = sp_[0][0]
                if n:
                    split_hi(next_tile + 1)
                    mean_root(n, r0)
                act.wait_ge(gain_ready, n + 1)
                for j in range(KC):
                    act.wait_ge(t_ready, n * INCS["t_ready"] + j + 1)
                    for a, b in sp_:
                        g = 0 if a == CTX else 1
                        m = own.mark(act.activation(nrm[:, j % 2, a:b], nrm[:, j % 2, a:b], ACT.Identity,
                                                    bias=mods[l][:, 3 * which, g, j:j + 1], scale=gain[l][:, which, g, j:j + 1]))
                    act.wait_ge(s_act, m)
                    act.activation(h_hi[:, j, r0:T], nrm[:, j % 2, r0:T], ACT.Copy).then_inc(h_hi_ready, 1)
                split_third_hi(next_tile + 2, which)

            act.wait_ge(zeroed, 6 + DEPTH)
            vectors(0)
            act.wait_ge(vec_ready, 1)
            act.activation(cond[:, :, :].rearrange("p c k -> p (c k)"), vecs[0][:, V_C:V_C + 16], ACT.Silu).then_inc(cond_ready, 1)
            for t in range(2, TT):
                load_tokens(t)
            for t in range(TT):
                act.wait_ge(xT_pe, 2 * t + 1)
                act.activation(x_res[:, 0:4, t * P:(t + 1) * P], banks[:, 2 * (t % 2), :].rearrange("p (k n) -> p k n", k=4),
                               ACT.Copy).then_inc(xT_a, 1)
            act.wait_ge(xT_a, TT)
            act.wait_ge(xT_b, TT)
            for j in range(KC):
                square_chunk(0, j, 0)
                if j == 1:
                    mod_rows_out(0)
            mean_root(0, 0)
            mod_rows_out(1)
            split_hi(0)
            split_hi(1)
            for l in range(DEPTH):
                base = tile_base[l]
                sp_ = spans(l)
                r0 = lat0(l)
                norm(l, 0, [(0, CTX), (CTX, T)], base)
                act.wait_ge(h_lo_ready, (2 * l) * INCS["h_lo_ready"] + KC)
                act.dma_start(inv_n[:, :], count[0]).then_inc(count_landed, 16)

                def silu_xbc(k):
                    act.wait_ge(pair_free[k % 2], pair_use(base + 2 + k) + 1)
                    acc = conv_acc[:, k % 2, :]
                    if k < 2:
                        act.activation(x_T[:, k, :], acc, ACT.Silu).then_inc(xbc_ready, 1)
                    elif k == 2:
                        act.activation(b_T[:, :], acc, ACT.Silu).then_inc(xbc_ready, 1)
                    else:
                        act.activation(c_T[0:64, 0, :], conv_acc[0:64, k % 2, :], ACT.Silu).then_inc(xbc_ready, 1)
                        act.activation(c_T[64:P, 1, :], conv_acc[64:P, k % 2, :], ACT.Silu).then_inc(xbc_ready, 1)

                for n in range(N_FEAT):
                    N = base + n
                    if n >= 2:
                        split_hi(N + 1)
                    if n < 2:
                        act.wait_ge(tile_done, N + 1)
                        if l < DEPTH - 1:
                            act.activation(pool_u[:, n, PC0:PC0 + CTX], bank_of(n % 2, 0, CTX), ACT.Copy)
                        act.activation(pool_u[:, n, PL0:PL0 + SEQ], bank_of(n % 2, CTX, T), ACT.Copy).then_inc(pair_free[n % 2], 1)
                    if 3 <= n <= 6:
                        silu_xbc(n - 3)
                    if n == 4 and l == 0:
                        vectors(1)
                        act.wait_ge(small_landed, 16 * 9 * DEPTH)
                        for k in range(DEPTH):
                            act.activation(neg_a[k][:, :], neg_a[k][:, :], ACT.Exp).then_inc(small_act, 1)
                    if n == 4:
                        act.wait_ge(count_used, l * INCS["count_used"] + 1)
                        act.dma_start(inv_n[:, :], count[1]).then_inc(count_landed, 16)
                    if n % 4 == 3:
                        mod_rows_out(l * N_MOD + 2 + n // 4)
                    if n >= 6:
                        act.wait_ge(tile_done, N + 1)
                        act.activation(silu_z[:, n - 6, r0:T], bank_of(n % 2, r0, T), ACT.Silu).then_inc(pair_free[n % 2], 1)
                def head_root(seq):
                    h0 = 2 * tok_from(l, 2) if seq else 0
                    act.wait_ge(qkss_ready, l * INCS["qkss_ready"] + seq + 1)
                    act.activation(qk_rt[:, seq, h0:12], qk_ss[:, seq, h0:12], ACT.Sqrt, bias=eps[:, 0:1],
                                   scale=1.0 / HEAD_DIM).then_inc(qkrt_ready, 1)

                for n in range(N_TOK):
                    N = base + N_FEAT + n
                    split_hi(N + 1)
                    st = n // 2
                    if n % 4 == 3:
                        mod_rows_out(l * N_MOD + 4 + n // 4)
                    if n == 2 or n == 6:
                        head_root(n // 4)
                    if n % 2 == 0:
                        continue
                    t0 = tok_from(l, st)
                    for t in range(t0, TT):
                        if t < TT - 1:
                            act.wait_ge(tok_ready, tok_count(l, st, True) + t - t0 + 1)
                        else:
                            act.wait_ge(tile_done, N + 1)
                        if st == 0:
                            act.activation(dt_raw[:, t, :], banks[:, t, 256:264], ACT.Copy)
                        dst = v_tok[:, t, :] if st == 1 else qk[:, (2, None, 0, 1)[st], t, :]
                        act.activation(dst, banks[:, t, 0:256], ACT.Copy).then_inc(tok_free, 1)
                    if st != 1:
                        seq = (0, None, 1, 2)[st]
                        act.wait_ge(tok_free, tok_count(l, st + 1))
                        if seq:
                            act.wait_ge(qkss_ready, l * INCS["qkss_ready"] + seq)
                        else:
                            act.wait_ge(pooled_ready, l * INCS["pooled_ready"] + 2)
                        act.activation(qk_sq[:, 2 * t0:12, :].rearrange("p a n -> p (a n)"),
                                       qk[:, (2, 0, 1)[seq], t0:TT, :].rearrange("p t n -> p (t n)"), ACT.Square).then_inc(qksq_ready, 1)
                    if st == 1:
                        act.wait_ge(dt_in, l * INCS["dt_in"] + 1)
                        act.activation(dt_n[:, :, :], dt_n[:, :, :], ACT.Exp).then_inc(dt_exp, 1)
                        act.wait_ge(dt_exp, l * INCS["dt_exp"] + 1)
                        act.activation(dt_n[:, :, :], dt_n[:, :, :], ACT.Ln, bias=ones[:, 0:1]).then_inc(dt_exp, 1)

                ev, units, two_buffers = mixer_events(l)
                nA = n_pv = n_y = n_gs = 0
                job_of = {}
                for e in ev:
                    if e == ("q23", 0):
                        head_root(2)
                    elif e[0] == "tr":
                        act.wait_ge(trA, l * INCS["trA"] + nA + 1)
                        src = banks[:, tr_bank(nA), :]
                        if e[1] == "x":
                            act.activation(x_tok[:, 0:4, e[2] * P:(e[2] + 1) * P], src.rearrange("p (t n) -> p t n", t=4), ACT.Copy).then_inc(trA_out, 1)
                        elif e[1] == "b":
                            act.activation(b_tok[:, 0:4, :], src.rearrange("p (t n) -> p t n", t=4), ACT.Copy).then_inc(trA_out, 1)
                        elif e[1] == "k":
                            act.activation(k_T[:, e[2], 0:512], src, ACT.Copy).then_inc(trA_out, 1)
                        else:
                            act.activation(q_T[:, e[2] % 2, CTX:T], src, ACT.Copy, scale=float(HEAD_DIM) ** -0.5).then_inc(trA_out, 1)
                        nA += 1
                    elif e[0] == "cs":
                        act.wait_ge(cs_pe, l * INCS["cs_pe"] + 1)
                        act.activation(decay[:, :, :, :].rearrange("p d c h -> p (d c h)"), banks[:, 7, 48:96], ACT.Exp).then_inc(cs_ready, 1)
                        act.activation(decay_all[:, :, :].rearrange("p c h -> p (c h)"), banks[:, 7, 96:144], ACT.Exp).then_inc(cs_ready, 1)
                        act.activation(cs_tok[:, :, :, :].rearrange("p d c h -> p (d c h)"), banks[:, 7, 0:48], ACT.Copy).then_inc(cs_ready, 1)
                    elif e[0] == "pool":
                        act.wait_ge(pm_pe, l * INCS["pm_pe"] + 2)
                        act.activation(mix[:, e[1], r0:T], bank_of(2 + e[1], r0, T),
                                       ACT.Copy, scale=vecs[l][:, V_PS + e[1]:V_PS + e[1] + 1]).then_inc(pm_out, 1)
                    elif e[0] == "exp":
                        u, (h, t) = e[1], e[2]
                        act.wait_ge(max_ready, l * INCS["max_ready"] + u + 1)
                        if u >= 3:
                            act.wait_ge(trA, l * INCS["trA"] + job_of[u - 3] + 1)
                        sb = score_bank(u, two_buffers)
                        if t < 0:
                            act.activation(probs[:, u % 3, 0:256], banks[:, sb, 0:256], ACT.Exp, bias=neg_max[:, u % 2, 0:1],
                                           accum_out=p_sum[:, u % 2, 0:1])
                            act.activation(probs[:, u % 3, 256:512], banks[:, sb, 256:512], ACT.Exp, bias=neg_max[:, u % 2, 1:2],
                                           accum_out=p_sum[:, u % 2, 1:2]).then_inc(exp_ready, 1)
                        else:
                            act.activation(probs[:, u % 3, :], flat[:, 512 * sb:512 * sb + T], ACT.Exp, bias=neg_max[:, u % 2, 0:1],
                                           accum_out=p_sum[:, u % 2, 0:1]).then_inc(exp_ready, 1)
                    elif e[0] == "trP":
                        u, (h, t) = e[1], e[2]
                        job_of[u] = nA
                        act.wait_ge(trA, l * INCS["trA"] + nA + 1)
                        if u >= 2:
                            act.wait_ge(pv_pe, l * INCS["pv_pe"] + u - 1)
                        if t < 0:
                            act.activation(p_T[:, u % 2, 0:4, :].rearrange("p (k q) n -> p q k n", q=2),
                                           banks[:, 2, :].rearrange("p (q k n) -> p q k n", q=2, k=2), ACT.Copy).then_inc(trA_out, 1)
                        else:
                            act.activation(p_T[:, u % 2, 0:4, :], banks[:, 2, :].rearrange("p (k n) -> p k n", k=4), ACT.Copy).then_inc(trA_out, 1)
                        nA += 1
                    elif e[0] == "PV":
                        u, (h, t) = e[1], e[2]
                        if t < 0 or t == SEQ // P - 1:
                            a, b = (0, CTX) if t < 0 else (CTX, T)
                            act.wait_ge(pv_pe, l * INCS["pv_pe"] + u + 1)
                            act.activation(mix[:, 4 + h, a:b], banks[:, 7, 0:b - a], ACT.Copy).then_inc(pv_out, 1)
                            n_pv += 1
                    elif e[0] == "ssd":
                        cc = e[1]
                        if n_y:
                            act.wait_ge(y_pe, l * INCS["y_pe"] + n_y)
                        for d in range(DIRS):
                            act.wait_ge(cb_pe, l * INCS["cb_pe"] + 2 * n_y + d + 1)
                            act.activation(e_cum[:, d, :, :].rearrange("p h s -> p (h s)"), banks[:, 5 - d, :], ACT.Exp).then_inc(ecum_ready, 1)
                        for h in range(HEADS):
                            ins = act.activation(e_in[:, 1, h, :], banks[:, 4, h * P:(h + 1) * P], ACT.Relu,
                                                 bias=cs_tok[:, 1, cc, h:h + 1], scale=-1.0)
                        ins.then_inc(d_back_ready, 1)
                        act.wait_ge(d_ready, l * INCS["d_ready"] + n_y + 1)
                        act.activation(e_in[:, 0, :, :], e_in[:, 0, :, :], ACT.Exp).then_inc(e_ready, 1)
                        act.wait_ge(d_back_ready, l * INCS["d_back_ready"] + n_y + 1)
                        act.activation(e_in[:, 1, :, :], e_in[:, 1, :, :], ACT.Exp, scale=-1.0).then_inc(e_ready, 1)
                        n_y += 1
                    elif e[0] == "gz":
                        act.wait_ge(gz_ready, l * INCS["gz_ready"] + e[1] + 1)
                        if e[1]:
                            act.wait_ge(gss_pe, l * INCS["gss_pe"] + len(sp_))
                        act.activation(gn_sq[:, r0:T], mix[:, 2 + e[1], r0:T], ACT.Square).then_inc(gsq_ready, 1)
                    elif e[0] == "gs":
                        a, b = sp_[e[2]]
                        act.wait_ge(gss_pe, l * INCS["gss_pe"] + n_gs + 1)
                        act.activation(gn_r[:, e[1], a:b], banks[:, 6, 0:b - a], ACT.Copy).then_inc(gss_out, 1)
                        n_gs += 1
                    elif e[0] == "gr":
                        act.wait_ge(gss_out, l * INCS["gss_out"] + n_gs)
                        act.activation(gn_r[:, :, r0:T], gn_r[:, :, r0:T], ACT.Sqrt, bias=eps[:, 0:1], scale=1.0 / P).then_inc(groot_ready, 1)
                act.wait_ge(gn_done, l * INCS["gn_done"] + 2 * (T - r0) // 256)
                act.wait_ge(pv_out, l * INCS["pv_out"] + n_pv)
                for j in range(KC):
                    act.activation(h_hi[:, j, r0:T], mix[:, j, r0:T], ACT.Copy).then_inc(m_hi_ready, 1)

                for n in range(N_OUT):
                    split_hi(base + N_FEAT + N_TOK + n + 1)
                    act.wait_ge(pair_free[n % 2], pair_use(base + N_FEAT + N_TOK + n) + 1)
                    square_chunk(2 * l + 1, n, r0)
                norm(l, 1, sp_, up_base[l][0])
                for b, nf in enumerate(FF_BLOCKS):
                    nb = up_base[l][b]
                    gb = (l * sum(FF_BLOCKS) + sum(FF_BLOCKS[:b]))

                    def up(i, first=False, mod_part=None):
                        for j in range(4):
                            if not first or j >= 2:
                                split_hi(nb + j + 1, i * 4)
                            if j == 3 and mod_part is not None:
                                mod_rows_out(mod_part)
                            m = pair_use(nb + j)
                            if j % 2 == 0:
                                act.wait_ge(tile_done, i * 4 + (nb + j + 1))
                                act.activation(silu_a[:, r0:T], bank_of(0, r0, T), ACT.Silu).then_inc(pair_free[0], 1)
                            else:
                                f = j // 2
                                act.wait_ge(pair_free[1], i * 2 + (m + 1))
                                act.activation(g_hi[:, bass.ds(i * (2 * T) + f * T + r0, T - r0)],
                                               g_f[:, f, r0:T], ACT.Copy).then_inc(g_hi_ready, 1)
                    at = 0
                    if b == 0:
                        up(0, True, (l + 1) * N_MOD if l < DEPTH - 1 else None)
                        at = 1
                        if l < DEPTH - 1:
                            up(1, False, (l + 1) * N_MOD + 1)
                            at = 2
                    with act.Fori(at, nf // 2) as i:
                        up(i)
                    last = b == len(FF_BLOCKS) - 1

                    def out_chunk(j):
                        act.wait_ge(o_pe, j + 1)
                        act.activation(x_out[:, j, :, :], banks[:, 4 + j % 2, :].rearrange("p (t n) -> p t n", n=P), ACT.Copy)\
                            .then_inc(out_ready, 1)
                    for n in range(KC):
                        N = down_base[l][b] + n
                        if N + 1 < DEPTH * N_TILES:
                            split_hi(N + 1)
                        if last and l == DEPTH - 1 and n >= 2:
                            out_chunk(n - 2)
                        if last and l < DEPTH - 1:
                            act.wait_ge(pair_free[n % 2], pair_use(N) + 1)
                            square_chunk(2 * l + 2, n, 0)
            for j in (KC - 2, KC - 1):
                out_chunk(j)

        @block.vector
        def _(dve):
            own = OwnOrder(s_dve)

            def link(ins):
                dve.wait_ge(s_dve, own.mark(ins))

            def as_f32(ap):
                return ap.bitcast(F32)

            def split_lo(n, i4=0):
                dve.wait_ge(hi_ready, i4 + (n + 1))
                dve.tensor_tensor(w_lo[n % 2][:, :], raw[n % 4][:, :], as_f32(w_hi[n % 2][:, :]), ALU.subtract).then_inc(lo_ready, 1)

            def split_third_lo(n, which):
                dve.wait_ge(hi_ready, n + 1)
                dve.tensor_tensor(w3_lo[which][:, :], raw[n % 4][:, :], as_f32(w3_hi[which][:, :]), ALU.subtract).then_inc(lo_ready, 1)

            def mod_bias(l, part):
                q = l * N_MOD + part
                dve.wait_ge(rows_T, q + 1)
                for t in range(2):
                    rows = banks[:, 6, P * t:P * t + P].rearrange("p (g r) -> p r g", g=4)[:, 0:2, :]
                    v0 = V_BMOD + KC * part + t
                    bias = vecs[l][:, v0:v0 + 7:2].unsqueeze(1).to_broadcast([P, 2, 4])
                    dve.tensor_tensor(mods[l][:, part, :, t:KC:2], rows, bias, ALU.add).then_inc(mods_ready, 1)

            def make_gain(l, which):
                dve.wait_ge(mods_ready, 2 * (l * N_MOD + 2 + 3 * which))
                v0 = (V_N1, V_N2)[which]
                dve.scalar_tensor_tensor(gain[l][:, which, :, :], mods[l][:, 1 + 3 * which, :, :], 1.0,
                                         vecs[l][:, v0:v0 + KC].unsqueeze(1).to_broadcast([P, 2, KC]),
                                         ALU.add, ALU.mult).then_inc(gain_ready, 1)

            def root_inverse(n, r0):
                dve.wait_ge(root_ready, n * INCS["root_ready"] + 1)
                w = (T - r0) // 4
                dve.reciprocal(rstd[:, 0:w], rstd[:, 0:w]).then_inc(rstd_ready, 1)

            def norm(l, which, sp_, next_tile):
                n = 2 * l + which
                r0 = sp_[0][0]
                if n:
                    split_lo(next_tile + 1)
                    root_inverse(n, r0)

                dve.wait_ge(rstd_pe, n * INCS["rstd_pe"] + 1)

                def low(j):
                    dve.wait_ge(h_hi_ready, n * INCS["h_hi_ready"] + j + 1)
                    dve.tensor_tensor(h_lo[:, j, r0:T], nrm[:, j % 2, r0:T], as_f32(h_hi[:, j, r0:T]), ALU.subtract)\
                        .then_inc(h_lo_ready, 1)
                for j in range(KC):
                    if j >= 2:
                        low(j - 2)
                        dve.wait_ge(h_lo_ready, n * KC + j - 1)
                    dve.tensor_tensor(nrm[:, j % 2, r0:T].rearrange("p (b n) -> p b n", b=2),
                                      x_res[:, j, r0:T].rearrange("p (b n) -> p b n", b=2), rstd_view(r0), ALU.mult).then_inc(t_ready, 1)
                low(KC - 2)
                low(KC - 1)
                split_third_lo(next_tile + 2, which)

            def gated_add(l, part, j, n, sp_):
                dve.wait_ge(tile_done, n + 1)
                for k, (a, b) in enumerate(sp_):
                    g = 0 if a == CTX else 1
                    ins = dve.scalar_tensor_tensor(x_res[:, j, a:b], bank_of(n % 2, a, b), mods[l][:, part, g, j:j + 1],
                                                   x_res[:, j, a:b], ALU.mult, ALU.add)
                    if k == len(sp_) - 1:
                        ins.then_inc(pair_free[n % 2], 1)

            for t in range(TT):
                dve.wait_ge(xT_pe, 2 * t + 2)
                dve.tensor_copy(x_res[:, 4:8, t * P:(t + 1) * P], banks[:, 2 * (t % 2) + 1, :].rearrange("p (k n) -> p k n", k=4))\
                    .then_inc(xT_b, 1)
            dve.wait_ge(vec_ready, 1)
            for j in range(1, KC - 1):
                dve.wait_ge(sq_ready, j + 1)
                if j > 1:
                    dve.wait_ge(acc_ready, j - 1)
                dve.tensor_tensor(sq_acc[:, :], sq[:, 0, :] if j == 1 else sq_acc[:, :], sq[:, j % 2, :], ALU.add).then_inc(acc_ready, 1)
                if j == 1:
                    mod_bias(0, 0)
            root_inverse(0, 0)
            mod_bias(0, 1)
            make_gain(0, 0)
            split_lo(0)
            split_lo(1)

            for l in range(DEPTH):
                base = tile_base[l]
                sp_ = spans(l)
                r0 = lat0(l)
                norm(l, 0, [(0, CTX), (CTX, T)], base)

                def conv(k):
                    N = base + 2 + k
                    dve.wait_ge(tile_done, N + 1)
                    if k >= 2:
                        dve.wait_ge(xbc_ready, l * INCS["xbc_ready"] + k - 1)
                    acc = conv_acc[:, k % 2, :]
                    streams = [(0, CTX), (CTX, T)]

                    def w(tap):
                        c0 = V_CW + 4 * tap + k
                        return vecs[l][:, c0:c0 + 1]
                    marks = []
                    for a, b in streams:
                        marks.append(own.mark(dve.tensor_scalar(acc[:, a:b], bank_of(N % 2, a, b), w(2),
                                                                vecs[l][:, V_CB + k:V_CB + k + 1], ALU.mult, ALU.add)))
                    for tap in (0, 1, 3, 4):
                        s = tap - 2
                        for q, (a, b) in enumerate(streams):
                            lo, hi = max(a, a - s), min(b, b - s)
                            dve.wait_ge(s_dve, marks[q])
                            ins = dve.scalar_tensor_tensor(acc[:, lo:hi], bank_of(N % 2, lo + s, hi + s), w(tap),
                                                           acc[:, lo:hi], ALU.mult, ALU.add)
                            if tap == 4 and q == 1:
                                ins.then_inc(pair_free[N % 2], 1)
                            else:
                                marks[q] = own.mark(ins)

                for n in range(N_FEAT):
                    if n >= 2:
                        split_lo(base + n + 1)
                    if 2 <= n < 6:
                        conv(n - 2)
                    if n == 4:
                        mod_bias(l, 2)
                    if n == 6 and l == 0:
                        dve.wait_ge(small_act, DEPTH)
                        for k in range(DEPTH):
                            dve.tensor_scalar(neg_a[k][:, :], neg_a[k][:, :], -1.0, None, ALU.mult).then_inc(small_ready, 1)
                            for half in range(2):
                                rows = slice(64 * half, 64 * half + 64)
                                dve.tensor_tensor(skip[k][rows, :], skip2[k][rows, half:HEADS:2],
                                                  skip2[k][rows, HEADS + half:2 * HEADS:2], ALU.add).then_inc(small_ready, 1)

                def first_head(seq):
                    return 2 * tok_from(l, 2) if seq else 0

                def reduce_heads(seq):
                    h0 = first_head(seq)
                    dve.wait_ge(qksq_ready, l * INCS["qksq_ready"] + seq + 1)
                    dve.tensor_reduce(qk_ss[:, seq, h0:12], qk_sq[:, h0:12, :], AX_X, ALU.add).then_inc(qkss_ready, 1)

                def scale_heads(seq):
                    h0 = first_head(seq)
                    dve.wait_ge(qkrt_ready, l * INCS["qkrt_ready"] + seq + 1)
                    link(dve.reciprocal(qk_rt[:, seq, h0:12], qk_rt[:, seq, h0:12]))
                    for k in range(h0, 12):
                        v = qk[:, (2, 0, 1)[seq], k // 2, P * (k % 2):P * (k % 2) + P]
                        ins = dve.scalar_tensor_tensor(v, v, qk_rt[:, seq, k:k + 1], qk_w[l][:, int(seq == 0), :],
                                                       ALU.mult, ALU.mult)
                    ins.then_inc(qkn_ready, 1)

                def rotate(seq):
                    dve.wait_ge(rope_s_ready, l * INCS["rope_s_ready"] + 2 * seq + 2)
                    v = qk[:, (2, 0, 1)[seq], 2:TT, :].rearrange("p t n -> p (t n)")
                    link(dve.tensor_tensor(v, v, rope_c, ALU.mult))
                    dve.tensor_tensor(v, v, rope_t[:, :], ALU.add).then_inc(qk_ready, 1)

                for n in range(N_TOK):
                    split_lo(base + N_FEAT + n + 1)
                    if n == 0:
                        mod_bias(l, 3)
                    if n == 4:
                        mod_bias(l, 4)
                        make_gain(l, 1)
                    if n == 2:
                        dve.wait_ge(tok_free, tok_count(l, 1))
                        link(dve.tensor_tensor(dt_raw[:, :, :], dt_raw[:, :, :],
                                               dt_b[l][:, :].unsqueeze(1).to_broadcast([P, TT, N_DT]), ALU.add))
                        link(dve.tensor_scalar(dt_m[:, :, :], dt_raw[:, :, :], 0.0, None, ALU.max))
                        link(dve.tensor_scalar(dt_n[:, :, :], dt_raw[:, :, :], 0.0, None, ALU.min))
                        dve.tensor_tensor(dt_n[:, :, :], dt_n[:, :, :], dt_m[:, :, :], ALU.subtract).then_inc(dt_in, 1)
                    if n == 5:
                        dve.wait_ge(dt_exp, l * INCS["dt_exp"] + 2)
                        link(dve.tensor_tensor(dts[:, :, :], dt_m[:, :, :], dt_n[:, :, :], ALU.add))
                        dve.tensor_tensor(a_tok[:, :, :], dts[:, :, :], neg_a[l][:, :].unsqueeze(1).to_broadcast([P, TT, N_DT]),
                                          ALU.mult).then_inc(a_ready, 1)
                    if n == 2 or n == 6:
                        reduce_heads(n // 4)
                    if n == 3 or n == 7:
                        scale_heads(n // 4)
                    if n == 4:
                        rotate(0)
                mod_bias(l, 5)

                ev, units, two_buffers = mixer_events(l)
                nA = nB = n_st = n_y = n_pv = 0
                scaled = -1

                def scale_probs(u, t):
                    dve.wait_ge(exp_ready, l * INCS["exp_ready"] + u + 1)
                    if t < 0:
                        link(dve.reciprocal(p_inv[:, u % 2, 0:2], p_sum[:, u % 2, 0:2]))
                        for q in range(2):
                            v = probs[:, u % 3, 256 * q:256 * q + 256]
                            ins = dve.tensor_scalar(v, v, p_inv[:, u % 2, q:q + 1], None, ALU.mult)
                        ins.then_inc(p_ready, 1)
                    else:
                        link(dve.reciprocal(p_inv[:, u % 2, 0:1], p_sum[:, u % 2, 0:1]))
                        v = probs[:, u % 3, :]
                        dve.tensor_scalar(v, v, p_inv[:, u % 2, 0:1], None, ALU.mult).then_inc(p_ready, 1)

                def y_evac(cc, k):
                    dve.wait_ge(y_pe, l * INCS["y_pe"] + k + 1)
                    if k == 0:
                        dve.wait_ge(qk_ready, l * INCS["qk_ready"] + 3)
                    for ft in range(2):
                        dve.scalar_tensor_tensor(mix[:, 2 + ft, cc * P:(cc + 1) * P], x_T[:, ft, cc * P:(cc + 1) * P],
                                                 skip[l][:, ft:ft + 1], banks[:, 6, ft * P:(ft + 1) * P],
                                                 ALU.mult, ALU.add).then_inc(y_out, 1)

                for e in ev:
                    if e == ("cs",):
                        rotate(1)
                    if e[0] == "q23":
                        if e[1] != 2:
                            (reduce_heads, scale_heads, None, rotate)[e[1]](2)
                    elif e[0] == "tr":
                        if e[1] != "q" or l < DEPTH - 1:
                            dve.wait_ge(trB, l * INCS["trB"] + nB + 1)
                            src = banks[:, tr_bank(nA) + 1, 0:256]
                            if e[1] == "x":
                                ins = dve.tensor_copy(x_tok[:, 4:6, e[2] * P:(e[2] + 1) * P], src.rearrange("p (t n) -> p t n", t=2))
                            elif e[1] == "b":
                                ins = dve.tensor_copy(b_tok[:, 4:6, :], src.rearrange("p (t n) -> p t n", t=2))
                            elif e[1] == "k":
                                ins = dve.tensor_copy(k_T[:, e[2], 512:T], src)
                            else:
                                ins = dve.tensor_scalar(q_T[:, e[2] % 2, 0:CTX], src, float(HEAD_DIM) ** -0.5, None, ALU.mult)
                            ins.then_inc(trB_out, 1)
                            nB += 1
                        nA += 1
                    elif e[0] == "cs":
                        dve.wait_ge(cs_ready, l * INCS["cs_ready"] + 1)
                        dve.tensor_tensor(w_state[:, :, :, :], decay[:, :, :, :],
                                          dts[:, :, :].rearrange("p c (d h) -> p d c h", d=DIRS), ALU.mult).then_inc(ws_ready, 1)
                        dve.wait_ge(cs_ready, l * INCS["cs_ready"] + 3)
                    elif e[0] == "state":
                        _, d, cc, nxt = e
                        first = cc == (0, 1)[d]
                        dst = h_prev[:, d, nxt, :].rearrange("p (h q) -> p h q", h=HEADS)
                        if n_st == 0:
                            dve.wait_ge(mod_used, KC * (l * N_MOD + N_MOD))
                        if first:
                            dve.wait_ge(st_pe, l * INCS["st_pe"] + n_st + 1)
                            dve.tensor_copy(h_prev[:, d, nxt, :], banks[:, 4 + n_st % 2, 0:256]).then_inc(st_ready, 1)
                        else:
                            dve.wait_ge(st_ready, l * INCS["st_ready"] + n_st - 1)
                            link(dve.tensor_tensor(dst, h_prev[:, d, cc, :].rearrange("p (h q) -> p h q", h=HEADS),
                                                   decay_all[:, cc, 4 * d:4 * d + 4].unsqueeze(2).to_broadcast([P, HEADS, HD_SSD]), ALU.mult))
                            dve.wait_ge(st_pe, l * INCS["st_pe"] + n_st + 1)
                            dve.tensor_tensor(h_prev[:, d, nxt, :], h_prev[:, d, nxt, :], banks[:, 4 + n_st % 2, 0:256], ALU.add)\
                                .then_inc(st_ready, 1)
                        n_st += 1
                    elif e[0] == "S":
                        u, (h, t) = e[1], e[2]
                        if u:
                            scale_probs(u - 1, units[u - 1][1])
                            scaled = u - 1
                        dve.wait_ge(s_ready, l * INCS["s_ready"] + u + 1)
                        sb = score_bank(u, two_buffers)
                        if t < 0:
                            dve.tensor_reduce(neg_max[:, u % 2, 0:2], banks[:, sb, :].rearrange("p (q n) -> p q n", q=2), AX_X,
                                              ALU.max, negate=True).then_inc(max_ready, 1)
                        else:
                            dve.tensor_reduce(neg_max[:, u % 2, 0:1], flat[:, 512 * sb:512 * sb + T], AX_X, ALU.max, negate=True).then_inc(max_ready, 1)
                    elif e[0] == "trP":
                        u, (h, t) = e[1], e[2]
                        if scaled < u:
                            scale_probs(u, t)
                            scaled = u
                        if t >= 0:
                            dve.wait_ge(trB, l * INCS["trB"] + nB + 1)
                            if u >= 2:
                                dve.wait_ge(pv_pe, l * INCS["pv_pe"] + u - 1)
                            dve.tensor_copy(p_T[:, u % 2, 4:6, :], banks[:, 3, 0:256].rearrange("p (k n) -> p k n", k=2))\
                                .then_inc(trB_out, 1)
                            nB += 1
                    elif e[0] == "ssd":
                        cc = e[1]
                        dve.wait_ge(ecum_ready, l * INCS["ecum_ready"] + 2 * n_y + 1)
                        for h in range(HEADS):
                            ins = dve.tensor_scalar(e_in[:, 0, h, :], banks[:, 5, h * P:(h + 1) * P], cs_tok[:, 0, cc, h:h + 1],
                                                    0.0, ALU.subtract, ALU.min)
                        ins.then_inc(d_ready, 1)
                        dve.wait_ge(g_pe, l * INCS["g_pe"] + n_y + 1)
                        for d, tri in ((0, tri_le), (1, tri_ge)):
                            dve.tensor_tensor(g_mask[:, d, :, :], banks[:, 6, 256:512].rearrange("p (g s) -> p g s", g=2),
                                              tri.unsqueeze(1).to_broadcast([P, 2, P]), ALU.mult).then_inc(gm_ready, 1)
                        n_y += 1
                    elif e[0] == "ssd_y":
                        dve.wait_ge(e_ready, l * INCS["e_ready"] + 2 * n_y - 1)
                        dve.wait_ge(gm_ready, l * INCS["gm_ready"] + 2 * n_y)
                        v = e_in[:, 0, :, :].rearrange("p (g r) s -> p g r s", r=2)
                        dve.tensor_tensor(v, v, g_mask[:, 0, :, :].unsqueeze(2).to_broadcast([P, 2, 2, P]), ALU.mult)\
                            .then_inc(w_ready, 1)
                        y_evac(e[1], n_y - 1)
                    elif e[0] == "gz":
                        dve.wait_ge(y_out, l * INCS["y_out"] + 2 * n_y)
                        v = mix[:, 2 + e[1], r0:T]
                        dve.tensor_tensor(v, v, silu_z[:, e[1], r0:T], ALU.mult).then_inc(gz_ready, 1)
                    elif e[0] == "gi":
                        ft, a = e[1], e[2]
                        dve.wait_ge(groot_ready, l * INCS["groot_ready"] + 1)
                        link(dve.reciprocal(gn_r[:, ft, a:a + 256], gn_r[:, ft, a:a + 256]))
                        v = mix[:, 2 + ft, a:a + 256]
                        dve.scalar_tensor_tensor(v, v, vecs[l][:, V_SN + ft:V_SN + ft + 1], gn_r[:, ft, a:a + 256], ALU.mult, ALU.mult)\
                            .then_inc(gn_done, 1)
                for j in range(KC):
                    dve.wait_ge(m_hi_ready, l * INCS["m_hi_ready"] + j + 1)
                    dve.tensor_tensor(h_lo[:, j, r0:T], mix[:, j, r0:T], as_f32(h_hi[:, j, r0:T]), ALU.subtract).then_inc(m_lo_ready, 1)

                for n in range(N_OUT):
                    N = base + N_FEAT + N_TOK + n
                    split_lo(N + 1)
                    gated_add(l, 2, n, N, sp_)
                norm(l, 1, sp_, up_base[l][0])
                for b, nf in enumerate(FF_BLOCKS):
                    nb = up_base[l][b]
                    gb = l * sum(FF_BLOCKS) + sum(FF_BLOCKS[:b])

                    def up(i, first=False):
                        m = pair_use(nb)

                        def g_low(f):
                            dve.wait_ge(g_hi_ready, i * 2 + (gb + f + 1))
                            at = bass.ds(i * (2 * T) + f * T + r0, T - r0)
                            dve.tensor_tensor(g_lo[:, at], g_f[:, f, r0:T], as_f32(g_hi[:, at]), ALU.subtract).then_inc(g_lo_ready, 1)
                        for j in range(4):
                            if not first or j >= 2:
                                split_lo(nb + j + 1, i * 4)
                            if j == 2:
                                g_low(0)
                            if j % 2:
                                f = j // 2
                                dve.wait_ge(pair_free[0], i * 2 + (m + f + 1))
                                dve.wait_ge(tile_done, i * 4 + (nb + j + 1))
                                dve.tensor_tensor(g_f[:, f, r0:T], silu_a[:, r0:T], bank_of(1, r0, T), ALU.mult)\
                                    .then_inc(pair_free[1], 1)
                        g_low(1)
                    at = 0
                    if b == 0:
                        up(0, True)
                        at = 1
                        if l < DEPTH - 1:
                            mod_bias(l + 1, 0)
                            up(1)
                            mod_bias(l + 1, 1)
                            make_gain(l + 1, 0)
                            at = 2
                    with dve.Fori(at, nf // 2) as i:
                        up(i)
                    for n in range(KC):
                        N = down_base[l][b] + n
                        if N + 1 < DEPTH * N_TILES:
                            split_lo(N + 1)
                        gated_add(l, 5, n, N, sp_)
        @block.tensor
        def _(pe):
            def mod_step(l, part, kc, i=0):
                q = l * N_MOD + part
                s = q * KC + kc
                if kc == 0:
                    if q > 0 or i > 0:
                        pe.wait_ge(rows_ready, i * 4 + 4 * q)
                pe.wait_ge(mod_landed[kc % 4], i * 32 + 16 * (s // 4 + 1))
                for g in range(4):
                    ins = pe.matmul(banks[32 * g:32 * g + 2, 7, 0:256], cond[:, :, kc], mod_ring[kc % 4][:, 256 * g:256 * g + 256],
                                    start=(kc == 0), stop=(kc == KC - 1))
                ins.then_inc(mod_used, 1)

            def mod_turn(l, part, i=0):
                q = l * N_MOD + part
                pe.wait_ge(rows_ready, i * 4 + 4 * (q + 1))
                if q > 0 or i > 0:
                    pe.wait_ge(mods_ready, i * 2 + 2 * q)
                for t in range(2):
                    ins = pe.transpose(banks[:, 6, P * t:P * t + P], mod_rows[:, P * t:P * t + P], ident)
                ins.then_inc(rows_T, 1)

            def sum_over_features(n, sp_):
                r0 = sp_[0][0]
                w = (T - r0) // 4
                pe.wait_ge(acc_ready, n * INCS["acc_ready"] + KC - 2)
                for g in range(4):
                    pe.matmul(banks[32 * g:32 * g + 32, 5, 0:w], ones[:, 0:32], sq_acc[:, r0 + g * w:r0 + g * w + w], start=True, stop=False)
                pe.wait_ge(sq_ready, n * INCS["sq_ready"] + KC)
                for g in range(4):
                    ins = pe.matmul(banks[32 * g:32 * g + 32, 5, 0:w], ones[:, 0:32], sq[:, (KC - 1) % 2, r0 + g * w:r0 + g * w + w],
                                    start=False, stop=True)
                ins.then_inc(ss_ready, 1)

            def spread_rstd(n, r0):
                w = (T - r0) // 4
                pe.wait_ge(rstd_ready, n * INCS["rstd_ready"] + 1)
                for g in range(4):
                    ins = pe.matmul(banks[:, 4 + g // 2, (g % 2) * w:(g % 2) * w + w], ident[:, 32 * g:32 * g + 1].to_broadcast([P, P]),
                                    rstd[:, 0:w], start=True, stop=True)
                ins.then_inc(rstd_pe, 1)

            def dense(n, x_hi, x_lo, n_k, sp_, i=0, chunk_ready=None, third=None):
                dense_tiles((n,), x_hi, x_lo, n_k, (sp_,), i, chunk_ready, third)

            def dense_tiles(tiles, x_hi, x_lo, n_k, spans_, i=0, chunk_ready=None, third=None):
                for n in tiles:
                    pe.wait_ge(lo_ready, i * 4 + (n + 1))
                    if pair_use(n) > 0 or i > 0:
                        pe.wait_ge(pair_free[n % 2], i * 2 + pair_use(n))
                for k in range(n_k):
                    if chunk_ready is not None:
                        pe.wait_ge(chunk_ready[0], chunk_ready[1] + k + 1)
                    w = slice(k * P, (k + 1) * P)
                    for n, sp_ in zip(tiles, spans_):
                        p = n % 2
                        hi, lo = (w_hi[p], w_lo[p]) if third is None else (w3_hi[third], w3_lo[third])
                        for q, (ws, xs) in enumerate(((hi, x_hi), (hi, x_lo), (lo, x_hi))):
                            for a, b in sp_:
                                ins = pe.matmul(bank_of(p, a, b), ws[:, w], xs(k, a, b), start=(k == 0 and q == 0),
                                                stop=(k == n_k - 1 and q == 2))
                        if k == n_k - 1:
                            ins.then_inc(tile_done, 1)

            def h_of(t):
                return lambda k, a, b: t[:, k, a:b]

            def g_of(t):
                return lambda k, a, b: t[:, k * T + a:k * T + b]

            def mod_steps(j, l, part, i=0):
                for s in range(STEPS_AT[j]):
                    mod_step(l, part, sum(STEPS_AT[:j]) + s, i)

            def vectors(l):
                pe.wait_ge(vrows_landed[l], 16 * (9 if l == 0 else 7))
                pe.transpose(banks[:, 4 + l, 0:N_VEC[l]], vrows[l][0:N_VEC[l], :], ident[0:N_VEC[l], 0:N_VEC[l]]).then_inc(vec_T, 1)

            pe.wait_ge(ident_landed, 16)
            vectors(0)
            pe.wait_ge(cond_ready, 1)
            slabs = [(part, kc) for part in range(2) for kc in range(KC)]
            for t in range(TT):
                pe.wait_ge(x_landed[t], 16)
                if t >= 2:
                    pe.wait_ge(xT_a, t - 1)
                    pe.wait_ge(xT_b, t - 1)
                for k in range(KC):
                    ins = pe.transpose(banks[:, 2 * (t % 2) + k // 4, (k % 4) * P:(k % 4 + 1) * P], x_in[:, t, k * P:(k + 1) * P], ident)
                    if k % 4 == 3:
                        ins.then_inc(xT_pe, 1)
                part, kc = slabs.pop(0)
                mod_step(0, part, kc)
            for part, kc in slabs:
                if part == 1 and kc == 5:
                    pe.wait_ge(table_landed, 16)
                    pe.wait_ge(xT_a, TT)
                    pe.wait_ge(xT_b, TT)
                    sum_over_features(0, [(0, CTX), (CTX, T)])
                mod_step(0, part, kc)
                if kc == KC - 1:
                    mod_turn(0, part)

            for l in range(DEPTH):
                base = tile_base[l]
                sp_ = spans(l)
                both = [(0, CTX), (CTX, T)]
                pe.wait_ge(mods_ready, 2 * (l * N_MOD + 2))
                if l:
                    sum_over_features(2 * l, both)
                if l:
                    mod_steps(0, l, 2)
                spread_rstd(2 * l, 0)
                dense_tiles((base, base + 1), h_of(h_hi), h_of(h_lo), KC, (sp_, sp_), chunk_ready=(h_lo_ready, 2 * l * KC))
                if l == 0:
                    mod_steps(0, l, 2)
                for n in range(2, N_FEAT):
                    dense(base + n, h_of(h_hi), h_of(h_lo), KC, both if n < 6 else sp_, third=0 if n == 2 else None)
                    mod_steps(n - 1 if n < 4 else n % 4, l, 2 + n // 4)
                    if n % 4 == 3:
                        mod_turn(l, 2 + n // 4)
                    if n == 3 and l == 0:
                        vectors(1)
                for p in range(2):
                    pe.wait_ge(pair_free[p], pair_use(base + N_FEAT))
                def token_blocks(i):
                    for j in range(4):
                        n = base + N_FEAT + j
                        st, half = 2 * i + j // 2, j % 2
                        width = 264 if st == 0 else 256
                        t0 = tok_from(l, st)
                        pe.wait_ge(lo_ready, i * 4 + (n + 1))
                        for t in range(t0, TT):
                            if half == 0 and (l, st) > (0, 0):
                                last_l, last_st = (l, st - 1) if st else (l - 1, 3)
                                pe.wait_ge(tok_free, tok_count(last_l, last_st) + t - tok_from(last_l, last_st) + 1)
                            for k in range(4):
                                kk = 4 * half + k
                                for q, (hs, ws) in enumerate(((h_hi, w_hi), (h_lo, w_hi), (h_hi, w_lo))):
                                    ins = pe.matmul(banks[:, t, 0:width], hs[:, kk, t * P:(t + 1) * P],
                                                    ws[n % 2][:, k * width:(k + 1) * width],
                                                    start=(kk == 0 and q == 0), stop=(kk == KC - 1 and q == 2))
                            if half == 1 and t < TT - 1:
                                ins.then_inc(tok_ready, 1)
                        ins.then_inc(tile_done, 1)
                        mod_steps(j, l, 4, i)
                    mod_turn(l, 4, i)
                for i in range(2):
                    token_blocks(i)

                ev, units, two_buffers = mixer_events(l)
                nA = nB = n_st = n_y = n_pv = n_gs = 0
                q_job, p_job = {}, {}
                pe.wait_ge(tok_free, tok_count(l, 4))
                pe.wait_ge(xbc_ready, l * INCS["xbc_ready"] + 5)

                def transposes(jobs):
                    nonlocal nA, nB
                    bank = tr_bank(nA)
                    prior = nA if nA >= 5 else nA - 1
                    if prior > 0:
                        pe.wait_ge(trA_out, l * INCS["trA_out"] + prior)
                        if nB:
                            pe.wait_ge(trB_out, l * INCS["trB_out"] + (nB if nA >= 5 else nB - 1))
                    for k, src in enumerate(jobs):
                        ins = pe.transpose(banks[:, bank + k // 4, (k % 4) * P:(k % 4 + 1) * P], src, ident)
                        if k == 3:
                            ins.then_inc(trA, 1)
                        elif k == 5:
                            ins.then_inc(trB, 1)
                    nA += 1
                    nB += len(jobs) > 4

                for e in ev:
                    if e[0] == "tr" and e[1] in ("x", "b"):
                        src = x_T[:, e[2], :] if e[1] == "x" else b_T[:, :]
                        transposes([src[:, t * P:(t + 1) * P] for t in range(TT)])
                    elif e[0] == "tr" and e[1] == "k":
                        pe.wait_ge(qk_ready, l * INCS["qk_ready"] + 1)
                        transposes([qk[:, 2, t, e[2] * P:(e[2] + 1) * P] for t in range(TT)])
                        k_job = nA, nB
                    elif e[0] == "tr":
                        pe.wait_ge(qk_ready, l * INCS["qk_ready"] + e[2] // 2 + 2)
                        q_job[e[2]] = nA + 1, nB + (l < DEPTH - 1)
                        order = [2, 3, 4, 5] + ([0, 1] if l < DEPTH - 1 else [])
                        transposes([qk[:, e[2] // 2, t, (e[2] % 2) * P:(e[2] % 2 + 1) * P] for t in order])
                    elif e[0] == "cs":
                        pe.wait_ge(a_ready, l * INCS["a_ready"] + 1)
                        pe.wait_ge(mods_ready, 2 * (l + 1) * N_MOD)
                        for col, tri, d in ((0, tri_le, 0), (24, tri_ge, 1), (48, tri_gt, 0), (72, tri_lt, 1)):
                            pe.matmul(banks[:, 7, col:col + 24], tri, a_tok[:, :, 4 * d:4 * d + 4], start=True, stop=True)
                        pe.matmul(banks[:, 7, 96:144], ones, a_tok[:, :, :], start=True, stop=True).then_inc(cs_pe, 1)
                    elif e[0] == "pool":
                        pe.wait_ge(cs_ready, l * INCS["cs_ready"] + 3)
                        pe.wait_ge(pooled_ready, l * INCS["pooled_ready"] + e[1] + 1)
                        pe.wait_ge(small_landed, 16 * 9 * DEPTH)
                        for a, b in sp_:
                            src = pool_u[:, e[1], PC0:PC0 + CTX] if a == 0 else pool_u[:, e[1], PL0:PL0 + SEQ]
                            ins = pe.matmul(bank_of(2 + e[1], a, b), pool_bd[l][:, e[1], :], src, start=True, stop=True)
                        ins.then_inc(pm_pe, 1)
                    elif e[0] == "state":
                        _, d, cc, nxt = e
                        pe.wait_ge(pm_out, l * INCS["pm_out"] + 2)
                        pe.wait_ge(xw_ready, l * INCS["xw_ready"] + n_st + 1)
                        if n_st >= 2:
                            pe.wait_ge(st_ready, l * INCS["st_ready"] + n_st - 1)
                        pe.matmul(banks[:, 4 + n_st % 2, 0:256], b_tok[:, cc, :], x_w[:, n_st % 2, :], start=True, stop=True)\
                            .then_inc(st_pe, 1)
                        n_st += 1
                    elif e[0] == "S":
                        u, (h, t) = e[1], e[2]
                        pe.wait_ge(trA_out, l * INCS["trA_out"] + max(q_job[h][0], k_job[0]))
                        pe.wait_ge(trB_out, l * INCS["trB_out"] + max(q_job[h][1], k_job[1]))
                        sb = score_bank(u, two_buffers)
                        if u == two_buffers:
                            pe.wait_ge(d_ready, l * INCS["d_ready"] + n_y)
                            pe.wait_ge(d_back_ready, l * INCS["d_back_ready"] + n_y)
                        elif u:
                            pe.wait_ge(exp_ready, l * INCS["exp_ready"] + (u if u < two_buffers else u - 1))
                        k_h = k_T[:, h // 2, :]
                        if t < 0:
                            for q in range(2):
                                ins = pe.matmul(banks[:, sb, 256 * q:256 * q + 256], q_T[:, h % 2, q * P:(q + 1) * P], k_h[:, 0:CTX],
                                                start=True, stop=True)
                        else:
                            q_t = q_T[:, h % 2, CTX + t * P:CTX + (t + 1) * P]
                            pe.matmul(banks[:, sb, :], q_t, k_h[:, 0:512], start=True, stop=True)
                            ins = pe.matmul(banks[:, sb + 1, 0:256], q_t, k_h[:, 512:T], start=True, stop=True)
                        ins.then_inc(s_ready, 1)
                    elif e[0] == "trP":
                        u, (h, t) = e[1], e[2]
                        pe.wait_ge(p_ready, l * INCS["p_ready"] + u + 1)
                        pv = probs[:, u % 3, :]
                        transposes([pv[:, k * P:(k + 1) * P] for k in range(4 if t < 0 else 6)])
                        p_job[u] = nA, nB
                    elif e[0] == "PV":
                        u, (h, t) = e[1], e[2]
                        pe.wait_ge(trA_out, l * INCS["trA_out"] + p_job[u][0])
                        pe.wait_ge(trB_out, l * INCS["trB_out"] + p_job[u][1])
                        if n_pv and t <= 0:
                            pe.wait_ge(pv_out, l * INCS["pv_out"] + n_pv)
                        g = h // 2
                        for k in range(2 if t < 0 else TT):
                            if t < 0:
                                dst, rhs = banks[:, 7, 0:CTX], p_T[:, u % 2, 2 * k:2 * k + 2, :].rearrange("p q n -> p (q n)")
                            else:
                                dst, rhs = banks[:, 7, t * P:(t + 1) * P], p_T[:, u % 2, k, :]
                            ins = pe.matmul(dst, v_tok[:, k, g * P:(g + 1) * P], rhs, start=(k == 0), stop=(k == (1 if t < 0 else TT - 1)))
                        ins.then_inc(pv_pe, 1)
                        n_pv += t < 0 or t == SEQ // P - 1
                    elif e[0] == "ssd":
                        cc = e[1]
                        if n_y == 0:
                            pe.wait_ge(pads_zero, l * INCS["pads_zero"] + 8)
                            pe.wait_ge(st_ready, l * INCS["st_ready"] + n_st)
                        for d in range(DIRS):
                            if n_y:
                                pe.wait_ge((d_ready, d_back_ready)[d], l * INCS["d_ready"] + n_y)
                            for h in range(HEADS):
                                ins = pe.matmul(banks[:, 5 - d, h * P:(h + 1) * P], a_tok[:, cc, 4 * d + h:4 * d + h + 1].to_broadcast([P, P]),
                                                (tri_le, tri_ge)[d], start=True, stop=True)
                            ins.then_inc(cb_pe, 1)
                        if n_y:
                            pe.wait_ge(y_out, l * INCS["y_out"] + 2 * n_y)
                        pe.matmul(banks[:, 6, 256:512].rearrange("p (g s) -> p g s", g=2), b_T[:, cc * P:(cc + 1) * P],
                                  c_T[:, :, cc * P:(cc + 1) * P], start=True, stop=True).then_inc(g_pe, 1)
                        n_y += 1
                    elif e[0] == "ssd_y":
                        cc = e[1]
                        pe.wait_ge(w_ready, l * INCS["w_ready"] + n_y)
                        pe.wait_ge(w_back_ready, l * INCS["w_back_ready"] + n_y)
                        pe.wait_ge(cdec_ready, l * INCS["cdec_ready"] + 2 * n_y)
                        for h in range(HEADS):
                            dst = banks[64 * (h % 2):64 * (h % 2) + 64, 6, (h // 2) * P:(h // 2 + 1) * P]
                            terms = [(x_dt[:, d, 64 * h:64 * h + 64], e_in[:, d, h, :]) for d in range(DIRS)]
                            terms += [(h_prev[:, d, cc, 64 * h:64 * h + 64], e_cum[:, d, h, :]) for d in range(DIRS) if cc != (0, 1)[d]]
                            for k, (lhs, rhs) in enumerate(terms):
                                ins = pe.matmul(dst, lhs, rhs, start=(k == 0), stop=(k == len(terms) - 1))
                        ins.then_inc(y_pe, 1)
                    elif e[0] == "gs":
                        a, b = sp_[e[2]]
                        pe.wait_ge(gsq_ready, l * INCS["gsq_ready"] + e[1] + 1)
                        if n_gs:
                            pe.wait_ge(gss_out, l * INCS["gss_out"] + n_gs)
                        else:
                            pe.wait_ge(y_out, l * INCS["y_out"] + 2 * n_y)
                        pe.matmul(banks[:, 6, 0:b - a], ones, gn_sq[:, a:b], start=True, stop=True).then_inc(gss_pe, 1)
                        n_gs += 1

                for n in range(0, N_OUT, 4):
                    for j in range(4):
                        dense(base + N_FEAT + N_TOK + n + j, h_of(h_hi), h_of(h_lo), KC, sp_,
                              chunk_ready=(m_lo_ready, l * KC) if n + j == 0 else None)
                sum_over_features(2 * l + 1, sp_)
                for b, nf in enumerate(FF_BLOCKS):
                    nb = up_base[l][b]

                    def up(i, with_mod=False, first=False):
                        if first:
                            if with_mod:
                                mod_steps(0, l + 1, 0, i)
                            spread_rstd(2 * l + 1, sp_[0][0])
                            dense_tiles((nb, nb + 1), h_of(h_hi), h_of(h_lo), KC, (sp_, sp_), i, (h_lo_ready, (2 * l + 1) * KC))
                        for j in range(2 if first else 0, 4):
                            dense(nb + j, h_of(h_hi), h_of(h_lo), KC, sp_, i, third=1 if first and j == 2 else None)
                            if with_mod:
                                mod_steps(j - 1 if first else j, l + 1, 0, i)
                        if with_mod:
                            mod_turn(l + 1, 0, i)
                    at = 0
                    if b == 0:
                        up(0, l < DEPTH - 1, True)
                        at = 1
                        if l < DEPTH - 1:
                            up(1, True)
                            at = 2
                    with pe.Fori(at, nf // 2) as i:
                        up(i)
                    hidden = (g_lo_ready, l * sum(FF_BLOCKS) + sum(FF_BLOCKS[:b]))
                    if l == DEPTH - 1 and b == len(FF_BLOCKS) - 1:
                        def transpose_out(j):
                            n = down_base[l][b] + j
                            pe.wait_ge(pair_free[n % 2], pair_use(n) + 1)
                            if j >= 2:
                                pe.wait_ge(out_ready, j - 1)
                            for t in range(SEQ // P):
                                ins = pe.transpose(banks[:, 4 + j % 2, t * P:(t + 1) * P], x_res[:, j, CTX + t * P:CTX + (t + 1) * P], ident)
                            ins.then_inc(o_pe, 1)

                        for j in range(KC):
                            dense(down_base[l][b] + j, g_of(g_hi), g_of(g_lo), nf, sp_, 0, hidden if j == 0 else None)
                            if j:
                                transpose_out(j - 1)
                        continue
                    with pe.Fori(0, 2) as i:
                        for j in range(4):
                            dense(down_base[l][b] + j, g_of(g_hi), g_of(g_lo), nf, sp_, i, hidden if j == 0 else None)
            transpose_out(KC - 1)


_INS = ['x', 'c', 'ctx', 'c_ctx', 'norm1_w', 'norm2_w', 'w_mod', 'b_mod', 'w_in', 'pool_w', 'pool_scale', 'conv_w', 'conv_b',
        'dt_bias', 'a_log', 'd_skip', 'ssd_norm_w', 'q_norm_w', 'k_norm_w', 'w_out', 'w1', 'w3', 'w2']
_OUTS = [((1, SEQ, D), 'float32')]


def kernel(**inputs):
    import numpy as _np
    import concourse.bacc as _bacc
    from concourse import mybir as _mybir
    from concourse.bass_utils import run_bass_kernel_spmd as _run

    nc = _bacc.Bacc("TRN2", target_bir_lowering=False, num_devices=1, dynamic_dma_scratch_size=1024)
    table, count = shape_constants()
    arrays, args = {}, []
    for name, a in [(n, inputs[n]) for n in _INS] + [("table", table), ("count", count)]:
        a = _np.ascontiguousarray(a)
        arrays[f"in_{name}_dram"] = a
        args.append(nc.dram_tensor(f"in_{name}_dram", a.shape, _mybir.dt.from_np(a.dtype), kind="ExternalInput").ap())
    for i, (shape, dtype) in enumerate(_OUTS):
        dt = _mybir.dt.from_np(_np.dtype(dtype))
        args.append(nc.dram_tensor(f"out_{i}_dram", shape, dt, kind="ExternalOutput").ap())
    hybrid_kernel(nc, *args)
    r = _run(nc, [arrays], core_ids=[0])
    got = tuple(r.results[0][f"out_{i}_dram"] for i in range(len(_OUTS)))
    return got[0]
```
